# Optimizing a Trainium2 kernel written in Bass

```python
import jax, jax.numpy as jnp
from jax import lax
import numpy as np

D_MODEL = 1024
BATCH = 1
SEQ = 512
DEPTH = 2
DEC_BATCH = 8
DEC_SEQ = 8
PAST_LEN = 4096
PAGE_SIZE = 128

N_META = 16
N_MIXERS = 2
SC_WIDTH = 3
CF_WIDTH = 31
D_SC = D_MODEL
D_CF = D_MODEL
N_GROUPS = 4
EXPERTS_PER_GROUP = 8
N_EXPERTS = N_GROUPS * EXPERTS_PER_GROUP
TOP_K = 2
D_EXPERT = D_MODEL // 4
ALPHA = float((2 * DEPTH) ** 0.25)
BETA = float((8 * DEPTH) ** -0.25)
N_A = (DEPTH + 1) // 2
N_B = DEPTH // 2
LN_EPS = 1e-5

kernel_name = "hybrid_shortconv_conformer_hmoe_step"

def layer_norm(x, g, b):
    xf = x.astype(jnp.float32)
    mu = xf.mean(-1, keepdims=True)
    var = jnp.square(xf - mu).mean(-1, keepdims=True)
    y = (xf - mu) * lax.rsqrt(var + LN_EPS)
    return (y * g.astype(jnp.float32) + b.astype(jnp.float32)).astype(x.dtype)

def causal_dwconv(full, w):
    return lax.conv_general_dilated(
        full, w[:, None, :].astype(full.dtype), window_strides=(1,), padding="VALID",
        dimension_numbers=("NWC", "WIO", "NWC"), feature_group_count=full.shape[-1])

def short_conv_mixer(h, hist, w_in, conv_w, w_out):
    bcv = jnp.einsum("btd,de->bte", h, w_in)
    b_gate, c_gate, v = jnp.split(bcv, 3, axis=-1)
    full = jnp.concatenate([hist.astype(h.dtype), c_gate * v], axis=1)
    conv = causal_dwconv(full, conv_w)
    y = jnp.einsum("btc,cd->btd", b_gate * conv, w_out)
    return y, full[:, -(SC_WIDTH - 1):]

def conformer_conv_mixer(h, hist, w1, b1, conv_w, conv_b, ln_g, ln_b, w2, b2):
    ag = jnp.einsum("btd,de->bte", h, w1) + b1
    a, g = jnp.split(ag, 2, axis=-1)
    full = jnp.concatenate([hist.astype(h.dtype), a * jax.nn.sigmoid(g)], axis=1)
    c = causal_dwconv(full, conv_w) + conv_b
    c = jax.nn.silu(layer_norm(c, ln_g, ln_b))
    y = jnp.einsum("btc,cd->btd", c, w2) + b2
    return y, full[:, -(CF_WIDTH - 1):]

def hierarchical_moe(h, rg_w, rg_b, re_w, re_b, w_gate, w_up, w_down):
    bsz, t, d = h.shape
    x = h.reshape(-1, d)
    glog = (x @ rg_w + rg_b).astype(jnp.float32)
    gprob = jax.nn.softmax(glog, axis=-1)
    gp, gidx = lax.top_k(gprob, 1)
    elog = (x @ re_w + re_b).astype(jnp.float32).reshape(-1, N_GROUPS, EXPERTS_PER_GROUP)
    sel = jnp.take_along_axis(elog, gidx[:, :, None], axis=1)[:, 0]
    eprob = jax.nn.softmax(sel, axis=-1)
    ew, eidx = lax.top_k(eprob, TOP_K)
    ew = ew / ew.sum(-1, keepdims=True)
    in_group = jnp.einsum("nk,nke->ne", ew, jax.nn.one_hot(eidx, EXPERTS_PER_GROUP, dtype=jnp.float32))
    grp = gp * jax.nn.one_hot(gidx[:, 0], N_GROUPS, dtype=jnp.float32)
    gate = (grp[:, :, None] * in_group[:, None, :]).reshape(-1, N_EXPERTS).astype(h.dtype)
    hid = jax.nn.silu(jnp.einsum("nd,edf->nef", x, w_gate)) * jnp.einsum("nd,edf->nef", x, w_up)
    out = jnp.einsum("nef,efd->nd", hid * gate[:, :, None], w_down)
    return out.reshape(bsz, t, d)

def run_trunk(h, st_a, st_b, sc_w_in, sc_conv_w, sc_w_out, cf_w_pw1, cf_b_pw1, cf_conv_w,
              cf_conv_b, cf_ln_g, cf_ln_b, cf_w_pw2, cf_b_pw2, ln1_g, ln1_b, ln2_g, ln2_b,
              rt_group_w, rt_group_b, rt_expert_w, rt_expert_b, moe_w_gate, moe_w_up, moe_w_down):
    new_a, new_b = [], []
    ia, ib = 0, 0
    for i in range(DEPTH):
        if i % N_MIXERS == 0:
            m, s = short_conv_mixer(h, st_a[ia], sc_w_in[ia], sc_conv_w[ia], sc_w_out[ia])
            new_a.append(s)
            ia += 1
        else:
            m, s = conformer_conv_mixer(h, st_b[ib], cf_w_pw1[ib], cf_b_pw1[ib], cf_conv_w[ib],
                                        cf_conv_b[ib], cf_ln_g[ib], cf_ln_b[ib], cf_w_pw2[ib], cf_b_pw2[ib])
            new_b.append(s)
            ib += 1
        h = layer_norm(ALPHA * h + m, ln1_g[i], ln1_b[i])
        f = hierarchical_moe(h, rt_group_w[i], rt_group_b[i], rt_expert_w[i], rt_expert_b[i],
                             moe_w_gate[i], moe_w_up[i], moe_w_down[i])
        h = layer_norm(ALPHA * h + f, ln2_g[i], ln2_b[i])
    return h, jnp.stack(new_a), jnp.stack(new_b)

def setup_inputs(seed: int = 0) -> dict:
    key = jax.random.key(seed)
    ks = jax.random.split(key, 32)
    f32 = jnp.float32
    nrm = lambda k, shape, s: jax.random.normal(k, shape, f32) * s
    d, F = D_MODEL, D_EXPERT
    return {
        "x_prompt": nrm(ks[0], (BATCH, SEQ, d), 1.0),
        "x_sample": nrm(ks[1], (DEC_BATCH, DEC_SEQ, d), 1.0),
        "state_conv_a": nrm(ks[2], (N_A, DEC_BATCH, SC_WIDTH - 1, D_SC), 1.0),
        "state_conv_b": nrm(ks[3], (N_B, DEC_BATCH, CF_WIDTH - 1, D_CF), 1.0),
        "meta_tokens": nrm(ks[4], (N_META, d), 1.0),
        "sc_w_in": nrm(ks[5], (N_A, d, 3 * D_SC), d ** -0.5),
        "sc_conv_w": nrm(ks[6], (N_A, SC_WIDTH, D_SC), SC_WIDTH ** -0.5),
        "sc_w_out": nrm(ks[7], (N_A, D_SC, d), BETA * D_SC ** -0.5),
        "cf_w_pw1": nrm(ks[8], (N_B, d, 2 * D_CF), d ** -0.5),
        "cf_b_pw1": nrm(ks[9], (N_B, 2 * D_CF), 0.02),
        "cf_conv_w": nrm(ks[10], (N_B, CF_WIDTH, D_CF), CF_WIDTH ** -0.5),
        "cf_conv_b": nrm(ks[11], (N_B, D_CF), 0.02),
        "cf_ln_g": 1.0 + nrm(ks[12], (N_B, D_CF), 0.02),
        "cf_ln_b": nrm(ks[13], (N_B, D_CF), 0.02),
        "cf_w_pw2": nrm(ks[14], (N_B, D_CF, d), BETA * D_CF ** -0.5),
        "cf_b_pw2": nrm(ks[15], (N_B, d), 0.02),
        "ln1_g": 1.0 + nrm(ks[16], (DEPTH, d), 0.02),
        "ln1_b": nrm(ks[17], (DEPTH, d), 0.02),
        "ln2_g": 1.0 + nrm(ks[18], (DEPTH, d), 0.02),
        "ln2_b": nrm(ks[19], (DEPTH, d), 0.02),
        "rt_group_w": nrm(ks[20], (DEPTH, d, N_GROUPS), d ** -0.5),
        "rt_group_b": nrm(ks[21], (DEPTH, N_GROUPS), 0.01),
        "rt_expert_w": nrm(ks[22], (DEPTH, d, N_EXPERTS), d ** -0.5),
        "rt_expert_b": nrm(ks[23], (DEPTH, N_EXPERTS), 0.01),
        "moe_w_gate": nrm(ks[24], (DEPTH, N_EXPERTS, d, F), d ** -0.5),
        "moe_w_up": nrm(ks[25], (DEPTH, N_EXPERTS, d, F), d ** -0.5),
        "moe_w_down": nrm(ks[26], (DEPTH, N_EXPERTS, F, d), BETA * F ** -0.5),
    }

def reference(x_prompt, x_sample, state_conv_a, state_conv_b, meta_tokens, sc_w_in, sc_conv_w,
              sc_w_out, cf_w_pw1, cf_b_pw1, cf_conv_w, cf_conv_b, cf_ln_g, cf_ln_b, cf_w_pw2,
              cf_b_pw2, ln1_g, ln1_b, ln2_g, ln2_b, rt_group_w, rt_group_b, rt_expert_w,
              rt_expert_b, moe_w_gate, moe_w_up, moe_w_down):
    weights = (sc_w_in, sc_conv_w, sc_w_out, cf_w_pw1, cf_b_pw1, cf_conv_w, cf_conv_b, cf_ln_g,
               cf_ln_b, cf_w_pw2, cf_b_pw2, ln1_g, ln1_b, ln2_g, ln2_b, rt_group_w, rt_group_b,
               rt_expert_w, rt_expert_b, moe_w_gate, moe_w_up, moe_w_down)
    bsz = x_prompt.shape[0]
    meta = jnp.broadcast_to(meta_tokens.astype(x_prompt.dtype)[None], (bsz, N_META, D_MODEL))
    hp = jnp.concatenate([meta, x_prompt], axis=1)
    zero_a = jnp.zeros((N_A, bsz, SC_WIDTH - 1, D_SC), x_prompt.dtype)
    zero_b = jnp.zeros((N_B, bsz, CF_WIDTH - 1, D_CF), x_prompt.dtype)
    hp, new_a_p, new_b_p = run_trunk(hp, zero_a, zero_b, *weights)
    y_prompt = hp[:, N_META:]
    hs, new_a_s, new_b_s = run_trunk(x_sample, state_conv_a, state_conv_b, *weights)
    return (y_prompt, hs, new_a_p, new_b_p, new_a_s, new_b_s)


_drawn_inputs = setup_inputs


def setup_inputs(seed=0):
    import zlib

    import numpy as np

    out = dict(_drawn_inputs(seed))
    spreads = {}
    factors = {'cf_conv_b': 5.497,
     'cf_ln_g': 17.641,
     'cf_ln_b': 37.373,
     'cf_b_pw2': 16.217,
     'rt_group_b': 114.414,
     'rt_expert_b': 6.693}
    for name, (base, spread) in spreads.items():
        noise = np.random.default_rng([zlib.crc32(name.encode()), seed]).standard_normal(out[name].shape)
        drawn = base * np.exp(spread * noise) if base else spread * noise
        out[name] = __import__('jax').numpy.asarray(drawn.astype(out[name].dtype))
    for name, factor in factors.items():
        out[name] = (out[name] * factor).astype(out[name].dtype)
    return out
```

```python
from contextlib import ExitStack

import concourse.bass as bass
from concourse import mybir

ALU = mybir.AluOpType
ACT = mybir.ActivationFunctionType
F32 = mybir.dt.float32
F32R = mybir.dt.float32r
I32 = mybir.dt.int32
U32 = mybir.dt.uint32
BF16 = mybir.dt.bfloat16
AX = mybir.AxisListType.X

P = 128
BANK = 512
ALPHA = 4.0 ** 0.25
LN_EPS = 1e-5


def build_decoder_step(nc, x_prompt, x_sample, state_a, state_b, meta, sc_w_in, sc_conv_w, sc_w_out,
                       cf_w1, cf_b1, cf_conv_w, cf_conv_b, cf_ln_g, cf_ln_b, cf_w2, cf_b2,
                       ln1_g, ln1_b, ln2_g, ln2_b, rg_w, rg_b, re_w, re_b, w_gate, w_up, w_down,
                       y_prompt, y_sample, new_a_prompt, new_b_prompt, new_a_sample, new_b_sample):
    _, SEQ, D = x_prompt.shape
    NS, DS, _ = x_sample.shape
    META = meta.shape[0]
    DEPTH, E, _, F = w_gate.shape
    G = rg_w.shape[2]
    EG = E // G
    KA, KB = sc_conv_w.shape[1], cf_conv_w.shape[1]
    HA, HB = KA - 1, KB - 1
    NP = META + SEQ
    T = NP + NS * DS
    NT = -(-T // P)
    ROWS = [min(P, T - t * P) for t in range(NT)]
    C = D // P
    HALF = T // 2
    PH = NP - HALF
    assert NP > HALF and NP - (NT - 1) * P == META and T % 2 == 0 and HALF <= BANK
    WA = HA + NP
    LA = WA + NS * (HA + DS)
    WB = HB + NP
    LB = WB + NS * (HB + DS)
    SA = HA + NS * HA
    SB = HB + NS * DS
    PAIRS = 2 * T
    XROWS = PAIRS + P
    TILES = (PAIRS - E) // P + E
    TAB = 48
    assert TILES + 2 <= TAB <= P and PAIRS > 2 * P
    T_RANK, T_ROW, T_ROWS, T_EXPERT, T_RAW, T_UPTO, T_LAST = (i * TAB for i in range(7))
    EARLY = 2
    SLOT = 3 * C * F
    SLOTS = 4
    SHARED = SLOTS - 1
    assert E % SLOTS == 0
    WIN_BLOCKS = 2
    PW_BLOCKS = 3
    DH = D // 2

    with ExitStack() as ctx:
        def sb(name, shape, dt=F32):
            return ctx.enter_context(nc.sbuf_tensor(name, shape, dt))

        def sem(name):
            return ctx.enter_context(nc.semaphore(name))

        ps = ctx.enter_context(nc.psum_tensor("ps", [P, 8, BANK], F32))
        B_TURN, B_RANK, B_LOGIT = 6, 4, 5
        B_GU, B_HIDT, B_Y = 0, 1, 2

        DIAGS = 8
        ring = sb("ring", [P, SHARED * SLOT + C * T + DIAGS * P + C * SB])
        assert C * T + DIAGS * P + C * SB >= SLOT
        at = SHARED * SLOT
        mixT = ring[:, at:at + C * T].rearrange("p (c t) -> p c t", c=C)
        at += C * T
        diag = ring[:, at:at + DIAGS * P].rearrange("p (i c) -> p i c", i=DIAGS)
        at += DIAGS * P
        keep = ring[:, at:at + C * SB].rearrange("p (c s) -> p c s", c=C)
        h = sb("h", [P, NT, D])
        hT_hi = sb("hT_hi", [P, C, T], F32R)
        hT_lo = sb("hT_lo", [P, C, T], F32R)
        KC = C // 2
        w_hi = sb("w_hi", [P, 2, KC, P], F32R)
        w_lo = sb("w_lo", [P, 2, KC, P], F32R)
        work = sb("work", [P, 4640])
        stage = sb("stage", [P, D])
        lnp = sb("lnp", [P, 2, D])
        hist_a = sb("hist_a", [P, C, NS * HA])
        NV = KA * C + 2 * C + 3 * C
        cvec = sb("cvec", [P, NV + KB * C])
        rw = sb("rw", [P, DEPTH, C, G + E])
        rb = sb("rb", [P, DEPTH, G + E])
        ones16 = sb("ones16", [P, P], BF16)
        before16 = sb("before16", [P, P], BF16)
        pick16 = sb("pick16", [P, NT, E], BF16)
        ident = sb("ident", [P, P])
        ones = sb("ones", [P, P])
        eps = sb("eps", [P, 1])
        iota_p = sb("iota_p", [P, 2])
        iota_m = sb("iota_m", [P, EG])
        valid = sb("valid", [P, NT])
        logit = sb("logit", [P, NT, G + E])
        r_small = sb("r_small", [P, 24, NT])
        r_g = sb("r_g", [P, 3, NT, G])
        r_goh = sb("r_goh", [P, NT, G])
        pick = sb("pick", [P, 2, NT, E])
        gates = sb("gates", [P, 2, NT])
        posf = sb("posf", [P, 2, NT])
        posi = sb("posi", [P, 2 * NT], U32)
        cnt = sb("cnt", [P, 3, E])
        scan = sb("scan", [P, 2, 3, E // 2 + E])
        excl = sb("excl", [P, 3, E])
        tsum = sb("tsum", [P, 6, E])
        tcol = sb("tcol", [P, 6])
        tab = sb("tab", [1, T_LAST + 1], I32)
        bn = sb("bn", [P, NT, 2, 6])
        mv = sb("mv", [P, NT, 2])
        sd = sb("sd", [P, NT, 3])

        u_in = [work[:, i * LA:(i + 1) * LA] for i in range(2)]
        c_sb = [work[:, 2 * LA + i * T:2 * LA + (i + 1) * T] for i in range(2)]
        acc_a = work[:, 2 * LA + 2 * T:2 * LA + 2 * T + LA - HA]
        glu = [work[:, i * LB:(i + 1) * LB] for i in range(4)]
        sig = [work[:, 4 * LB + i * T:4 * LB + (i + 1) * T] for i in range(2)]
        mean_sb, rstd_sb = sig
        squares = [work[:, i * T:(i + 1) * T] for i in range(4)]
        PE_CONVS = (1, 4)
        DVE_CONVS = [j for j in range(C) if j not in PE_CONVS]
        glu_of = {j: glu[i % 2] for i, j in enumerate(DVE_CONVS)} | {j: glu[2 + i] for i, j in enumerate(PE_CONVS)}
        CUT = 20
        PLAN_B = [("P", 0), ("P", 1), ("P", 2), ("P", 3), ("C", 1, 0, CUT), ("P", 4), ("P", 5), ("C", 1, CUT, KB),
                  ("P", 6), ("P", 7), ("C", 4, 0, KB)]
        assert C == 8
        NHB = NS * HB // 2
        hb_rows = stage[0:NHB]
        x_rows = work[:, 0:D]
        xT = work[:, D:2 * D].rearrange("p (k n) -> p k n", n=P)
        y_rows = work[:, 2 * D:3 * D]
        silu_sb = work[:, 3 * D:3 * D + F]
        hid = work[:, 3 * D + F:3 * D + 2 * F]
        hidT = work[:, 3 * D + 2 * F:3 * D + 3 * F].rearrange("p (k n) -> p k n", n=P)
        FK = F // P
        picked = [v[:, 2 * D * b:2 * D * (b + 1)].rearrange("p (k d) -> p k d", k=2)
                  for v in (mixT[:].rearrange("p c t -> p (c t)"), work) for b in range(2)]
        NB = len(picked)
        r_e = work[:, 0:6 * NT * EG].rearrange("p (i t e) -> p i t e", t=NT, e=EG)
        r_pick = work[:, 512:512 + NT * E].rearrange("p (t e) -> p t e", e=E)
        r_pos = work[:, 1024:1024 + 2 * NT * E].rearrange("p (i t e) -> p i t e", t=NT, e=E)
        vrows = work[0:NV, 0:P]
        KBR = KB * C // 2
        cfrows = [work[0:KBR, P * (1 + i):P * (2 + i)] for i in range(2)]
        harows = work[0:NS * HA, 3 * P:3 * P + D]

        xs = [nc.dram_tensor(f"x_sorted{l}", (XROWS, D), F32).ap() for l in range(DEPTH)]
        ys = [nc.dram_tensor(f"y_sorted{l}", (XROWS, D), F32).ap() for l in range(DEPTH)]

        def sc_tap(k, j): return cvec[:, k * C + j:k * C + j + 1]
        def bias_a(j): return cvec[:, KA * C + j:KA * C + j + 1]
        def bias_g(j): return cvec[:, KA * C + C + j:KA * C + C + j + 1]
        def conv_b(j): return cvec[:, KA * C + 2 * C + j:KA * C + 2 * C + j + 1]
        def cln_g(j): return cvec[:, KA * C + 3 * C + j:KA * C + 3 * C + j + 1]
        def cln_b(j): return cvec[:, KA * C + 4 * C + j:KA * C + 4 * C + j + 1]
        def cf_tap(k, j): return cvec[:, NV + k * C + j:NV + k * C + j + 1]

        h_turn = h[:].rearrange("p t (q k) -> p t k q", k=C)

        def seqs(ap, width):
            return ap.rearrange("p (s w) -> p s w", w=width)

        h_loaded = [sem(f"h_loaded{t}") for t in range(NT)]
        rows_loaded = sem("rows_loaded")
        router_loaded = sem("router_loaded")
        lnp_loaded = sem("lnp_loaded")
        b2_loaded = sem("b2_loaded")
        pads_stored = sem("pads_stored")
        consts_made = sem("consts_made")
        iota_made = sem("iota_made")
        zeros_made = sem("zeros_made")
        rows_turned = sem("rows_turned")
        rows_act = sem("rows_act")
        w_hi_ready, w_lo_ready, w_used = sem("w_hi_ready"), sem("w_lo_ready"), sem("w_used")
        diag_ready, diag_used = sem("diag_ready"), sem("diag_used")
        pe_conv_done, pe_conv_read = sem("pe_conv_done"), sem("pe_conv_read")
        hist_loaded, hist_turned, hist_read = sem("hist_loaded"), sem("hist_turned"), sem("hist_read")
        squares_used = sem("squares_used")
        slot_loaded = [sem(f"slot_loaded{i}") for i in range(SLOTS)]
        weights_ready = sem("weights_ready")
        mixer_slots_used = sem("mixer_slots_used")
        h_turned = sem("h_turned")
        hT_act, hT_dve = sem("hT_act"), sem("hT_dve")
        q_done = sem("q_done")
        c_copied, cv_done, a_mixed = sem("c_copied"), sem("cv_done"), sem("a_mixed")
        kept = sem("kept")
        g_done = sem("g_done")
        sig_done, glu_done, b_step = sem("sig_done"), sem("glu_done"), sem("b_step")
        conv_step, conv_done = sem("conv_step"), sem("conv_done")
        sums_done, mean_ready, centred, squared = sem("sums_done"), sem("mean_ready"), sem("centred"), sem("squared")
        vars_done, csd_ready, normed, b_mixed = sem("vars_done"), sem("csd_ready"), sem("normed"), sem("b_mixed")
        state_turned, state_act, state_out = sem("state_turned"), sem("state_act"), sem("state_out")
        proj_done, z_done = sem("proj_done"), sem("z_done")
        h_scaled = sem("h_scaled")
        h_mul = sem("h_mul")
        var_ready, sd_ready, rstd_ready = sem("var_ready"), sem("sd_ready"), sem("rstd_ready")
        ln_applied, ln_gained, ln_done = sem("ln_applied"), sem("ln_gained"), sem("ln_done")
        logits_done, logits_read = sem("logits_done"), sem("logits_read")
        exp_in, exp_out = sem("exp_in"), sem("exp_out")
        cols_ready, cols_turned = sem("cols_ready"), sem("cols_turned")
        picks_ready, ranked, pos_ready, tab_ready = sem("picks_ready"), sem("ranked"), sem("pos_ready"), sem("tab_ready")
        step_s = sem("dve_step")
        pool_step = sem("pool_step")
        scattered = sem("scattered")
        L = range(DEPTH)
        x_loaded = [sem(f"x_loaded{l}") for l in L]
        x_turned = [sem(f"x_turned{l}") for l in L]
        xT_act = [sem(f"xT_act{l}") for l in L]
        xT_dve = [sem(f"xT_dve{l}") for l in L]
        gu_done = [sem(f"gu_done{l}") for l in L]
        silu_done = [sem(f"silu_done{l}") for l in L]
        hid_done = [sem(f"hid_done{l}") for l in L]
        hid_turned = [sem(f"hid_turned{l}") for l in L]
        hidT_ready = [sem(f"hidT_ready{l}") for l in L]
        y_done = [sem(f"y_done{l}") for l in L]
        y_act = [sem(f"y_act{l}") for l in L]
        y_dve = [sem(f"y_dve{l}") for l in L]
        y_stored = [sem(f"y_stored{l}") for l in L]
        ys_complete = sem("ys_complete")
        gathered = [sem(f"gathered{b}") for b in range(NB)]
        combined = sem("combined")
        out_stored = sem("out_stored")

        NWIN, NWOUT = C // WIN_BLOCKS, 2
        NPW, NPW2 = -(-C // PW_BLOCKS), 2
        MIX_SLOTS = [NWIN + NWOUT, NPW + NPW2]
        SEQ_MIX = [0, MIX_SLOTS[0] + E]
        SEQ_EXP = [MIX_SLOTS[0], MIX_SLOTS[0] + E + MIX_SLOTS[1]]

        MIX_PLACES = [(0, 1, 2), (1, 2, 0)]

        def place(n):
            layer = 0 if n < SEQ_MIX[1] else 1
            if n >= SEQ_EXP[layer]:
                return (n - SEQ_EXP[layer]) % SLOTS
            return MIX_PLACES[layer][(n - SEQ_MIX[layer]) % 3]

        def prior(n):
            return max((m for m in range(n) if place(m) == place(n)), default=None)

        class Product:

            def __init__(self, index, n, col, pitch, frees):
                self.index, self.n, self.col, self.pitch, self.frees = index, n, col, pitch, frees

        def products(layer):
            out = []
            for j in range(C):
                per = WIN_BLOCKS if layer == 0 else PW_BLOCKS
                nb = min(per, C - j // per * per)
                groups = 3 if layer == 0 else 2
                for r in range(groups):
                    out.append(Product(groups * j + r, SEQ_MIX[layer] + j // per, (r * nb + j % per) * P,
                                       groups * nb * P, r == groups - 1 and j % per == nb - 1))
            return out

        PRODUCTS = [products(0), products(1)]
        SPLITS = [0, 2 * len(PRODUCTS[0])]

        def raw_chunk(p, c):
            w = slot(p.n)[:, 0:C * p.pitch].rearrange("p (k c) -> p k c", k=C)
            return w[:, c * KC:(c + 1) * KC, p.col:p.col + P]

        LAG = 2

        def slot(n):
            return ring[:, place(n) * SLOT:(place(n) + 1) * SLOT]

        ring_gu = ring[:, 0:SLOTS * SLOT].rearrange("p (s u k c) -> p s u k c", s=SLOTS, u=3, k=C)
        ring_dn = ring[:, 0:SLOTS * SLOT].rearrange("p (s u k d) -> p s u k d", s=SLOTS, u=3, k=FK)

        def last_tile(eng):
            return eng.value_load(tab[0:1, T_LAST:T_LAST + 1], min_val=PAIRS // P - 1, max_val=TILES - 1)

        block = ctx.enter_context(nc.Block())

        @block.sync
        def _(sp):
            given = [0] * SLOTS

            def load_mixer(n, pieces):
                for dst, src in pieces:
                    sp.dma_start(dst, src).then_inc(slot_loaded[place(n)], 16)
                    given[place(n)] += 16

            def mixer_pieces(layer, i):
                n = SEQ_MIX[layer] + i
                s = slot(n)
                if layer == 0 and i < NWIN:
                    w = WIN_BLOCKS * P
                    v = s[:, 0:C * 3 * w].rearrange("p (k g c) -> p k g c", k=C, g=3)
                    src = sc_w_in[0].rearrange("(p k) (g c) -> p k g c", k=C, g=3)
                    return [(v[:, :, to, :], src[:, :, g, i * w:(i + 1) * w]) for to, g in ((0, 1), (1, 2), (2, 0))]
                if layer == 1 and i < NPW:
                    nb = min(PW_BLOCKS, C - i * PW_BLOCKS)
                    v = s[:, 0:C * 2 * nb * P].rearrange("p (k g c) -> p k g c", k=C, g=2)
                    src = cf_w1[0].rearrange("(p k) (g c) -> p k g c", k=C, g=2)
                    c0 = i * PW_BLOCKS * P
                    return [(v[:, :, to, :], src[:, :, g, c0:c0 + nb * P]) for to, g in ((0, 1), (1, 0))]
                half = i - (NWIN if layer == 0 else NPW)
                w2 = sc_w_out if layer == 0 else cf_w2
                v = s[:, 0:C * DH].rearrange("p (j n) -> p j n", j=C)
                return [(v, w2[0].rearrange("(j p) n -> p j n", p=P)[:, :, half * DH:(half + 1) * DH])]

            def load_expert(layer, r, number=None):
                s = ring[:, r % SLOTS * SLOT:(r % SLOTS + 1) * SLOT]
                u = C * F
                if number is None:
                    e, cond = r, {}
                else:
                    e = sp.value_load(tab[0:1, bass.ds(number + T_EXPERT, 1)], min_val=0, max_val=E - 1)
                    raw = sp.value_load(tab[0:1, bass.ds(number + T_RAW, 1)], min_val=0, max_val=E)
                    cond = dict(cond=raw < E)
                e1 = bass.ds(e, 1)
                for dst, src in ((s[:, 0:u], w_gate[layer, e1].rearrange("e (p k) f -> p (e k f)", k=C)),
                                 (s[:, u:2 * u], w_up[layer, e1].rearrange("e (p k) f -> p (e k f)", k=C)),
                                 (s[:, 2 * u:3 * u], w_down[layer, e1].rearrange("e (p k) d -> p (e k d)", k=FK))):
                    sp.dma_start(dst, src, **cond).then_inc(slot_loaded[r % SLOTS], 16)

            def pass_on(n):
                sp.wait_ge(slot_loaded[place(n)], given[place(n)])
                sp.sem_inc(weights_ready, 1)

            for layer in L:
                if layer > 0:
                    sp.wait_ge(tab_ready, layer)
                for i in range(MIX_SLOTS[layer] + SLOTS):
                    n = SEQ_MIX[layer] + i
                    if n >= LAG:
                        pass_on(n - LAG)
                    m = prior(n)
                    if i == MIX_SLOTS[layer] + EARLY:
                        sp.wait_ge(tab_ready, layer + 1)
                        sp.wait_ge(x_loaded[layer], 32)
                    if m is not None and place(n) != SHARED:
                        if layer > 0 and m < SEQ_MIX[layer]:
                            at = T_UPTO + m - SEQ_EXP[layer - 1]
                            upto = sp.value_load(tab[0:1, at:at + 1], min_val=0, max_val=TILES)
                            sp.wait_ge(y_done[layer - 1], upto + 1)
                        else:
                            used = sum(MIX_SLOTS[:layer]) + m - SEQ_MIX[layer] + 1
                            sp.wait_ge(mixer_slots_used, used)
                    if n == 1:
                        for t in range(NT):
                            sp.wait_ge(h_loaded[t], 16 if 0 < t < NT - 1 else 32)
                        sp.wait_ge(rows_loaded, 16 * 8)
                    if i < MIX_SLOTS[layer]:
                        load_mixer(n, mixer_pieces(layer, i))
                    else:
                        rank = i - MIX_SLOTS[layer]
                        load_expert(layer, rank, rank if rank >= EARLY else None)
                        given[place(n)] += 48
                base = list(given)
                with sp.Fori(1, E // SLOTS) as g:
                    for r in range(SLOTS):
                        behind = (r - LAG) % SLOTS
                        sofar = g * 48 - 48 + base[behind] if r < LAG else g * 48 + base[behind]
                        sp.wait_ge(slot_loaded[behind], sofar)
                        sp.sem_inc(weights_ready, 1)
                        upto = sp.value_load(tab[0:1, bass.ds(g * SLOTS + (T_UPTO + r - SLOTS), 1)],
                                             min_val=0, max_val=TILES)
                        sp.wait_ge(y_done[layer], upto + 1)
                        load_expert(layer, r, g * SLOTS + r)
                for r in range(SLOTS):
                    given[r] = base[r] + 48 * (E // SLOTS - 1)
            for i in range(LAG):
                pass_on(SEQ_EXP[-1] + E - LAG + i)

            for t in range(NT):
                sp.wait_ge(ln_done, NT * (2 * DEPTH - 1) + t + 1)
                lo = META if t == 0 else 0
                hi = META if t == NT - 1 else ROWS[t]
                r0 = t * P + lo - META
                sp.dma_start(y_prompt[0, r0:r0 + hi - lo, :], h[lo:hi, t, :]).then_inc(out_stored, 16)
                if t == NT - 1:
                    sp.dma_start(y_sample.rearrange("s t d -> (s t) d"), h[META:ROWS[t], t, :]).then_inc(out_stored, 16)
            sp.wait_ge(out_stored, 16 * (NT + 1))

        @block.scalar
        def _(act):
            act.dma_start(h[0:META, 0, :], meta).then_inc(h_loaded[0], 16)
            act.dma_start(h[META:P, 0, :], x_prompt[0, 0:P - META, :]).then_inc(h_loaded[0], 16)
            for t in range(1, NT - 1):
                act.dma_start(h[:, t, :], x_prompt[0, t * P - META:(t + 1) * P - META, :]).then_inc(h_loaded[t], 16)
            act.dma_start(h[0:META, NT - 1, :], x_prompt[0, SEQ - META:SEQ, :]).then_inc(h_loaded[NT - 1], 16)
            act.dma_start(h[META:META + NS * DS, NT - 1, :],
                          x_sample.rearrange("s t d -> (s t) d")).then_inc(h_loaded[NT - 1], 16)
            at = 0
            for v in (sc_conv_w[0].rearrange("k (j c) -> (k j) c", c=P),
                      cf_b1[0:1].rearrange("o (j c) -> (o j) c", c=P),
                      cf_conv_b[0:1].rearrange("o (j c) -> (o j) c", c=P),
                      cf_ln_g[0:1].rearrange("o (j c) -> (o j) c", c=P),
                      cf_ln_b[0:1].rearrange("o (j c) -> (o j) c", c=P)):
                n = v.shape[0]
                act.dma_start(vrows[at:at + n, :], v).then_inc(rows_loaded, 16)
                at += n
            taps = cf_conv_w[0].rearrange("k (j c) -> (k j) c", c=P)
            hb_dram = state_b[0].rearrange("s r d -> (s r) d")
            for i in range(2):
                act.dma_start(cfrows[i], taps[i * KBR:(i + 1) * KBR, :]).then_inc(rows_loaded, 16)
            act.dma_start(harows, state_a[0].rearrange("s r d -> (s r) d")).then_inc(rows_loaded, 16)
            for l in L:
                act.dma_start(rw[:, l, :, 0:G], rg_w[l].rearrange("(p k) g -> p k g", k=C)).then_inc(router_loaded, 16)
                act.dma_start(rw[:, l, :, G:G + E], re_w[l].rearrange("(p k) e -> p k e", k=C)).then_inc(router_loaded, 16)
                act.dma_start(rb[:, l, 0:G], rg_b[l].partition_broadcast(P)).then_inc(router_loaded, 16)
                act.dma_start(rb[:, l, G:G + E], re_b[l].partition_broadcast(P)).then_inc(router_loaded, 16)
            act.dma_start(new_b_sample[0, :, 0:HB - DS, :], state_b[0, :, DS:HB, :]).then_inc(state_out, 16)

            def load_ln_params(i):
                gp, bp = ((ln1_g, ln1_b), (ln2_g, ln2_b))[i % 2]
                act.dma_start(lnp[:, 0, :], gp[i // 2].partition_broadcast(P)).then_inc(lnp_loaded, 16)
                act.dma_start(lnp[:, 1, :], bp[i // 2].partition_broadcast(P)).then_inc(lnp_loaded, 16)

            load_ln_params(0)
            act.wait_ge(zeros_made, 1)
            for l in L:
                act.dma_start(xs[l][PAIRS:XROWS, :], stage[:]).then_inc(pads_stored, 16)

            def copy_hT(m):
                t, n = m % NT, ROWS[m % NT]
                act.wait_ge(h_turned, m + 1)
                for i in range(1 if m // NT % 2 else 2):
                    src = ps[:, B_TURN + i, :].rearrange("p (k n) -> p k n", n=P)[:, :, 0:n]
                    if m // NT % 2:
                        last = nc.scalar.copy(xT[:, 0:KC, 0:n], src)
                    else:
                        last = nc.scalar.copy(hT_hi[:, i * KC:(i + 1) * KC, t * P:t * P + n], src)
                last.then_inc(hT_act, 1)

            def split_hi(layer, p):
                act.wait_ge(weights_ready, p.n + 1)
                for c in range(2):
                    i = SPLITS[layer] + 2 * p.index + c
                    if i >= 2:
                        act.wait_ge(w_used, i - 1)
                    nc.scalar.copy(w_hi[:, i % 2], raw_chunk(p, c)).then_inc(w_hi_ready, 1)

            def scale_h(t, signal):
                nc.scalar.mul(h[0:ROWS[t], t, :], h[0:ROWS[t], t, :], ALPHA).then_inc(signal, 1)

            def normalise(m):
                t, n = m % NT, ROWS[m % NT]
                act.wait_ge(var_ready, m + 1)
                nc.scalar.activation(sd[0:n, t, 0:1], mv[0:n, t, 1:2], ACT.Sqrt, bias=eps[0:n, 0:1]).then_inc(sd_ready, 1)
                act.wait_ge(rstd_ready, m + 1)
                nc.scalar.activation(h[0:n, t, :], h[0:n, t, :], ACT.Identity, bias=sd[0:n, t, 2:3],
                                     scale=sd[0:n, t, 1:2]).then_inc(ln_applied, 1)

            def state_rows(layer, n):
                act.wait_ge(state_turned, layer + 1)
                if layer == 0:
                    act.wait_ge(pads_stored, 32)
                else:
                    act.wait_ge(hist_turned, 2)
                for i in range(2):
                    last = nc.scalar.copy(stage[0:n, i * DH:(i + 1) * DH], ps[0:n, 4 + i, :])
                last.then_inc(state_act, 1)
                act.wait_ge(state_act, layer + 1)

            def experts(l):
                act.wait_ge(tab_ready, l + 1)
                last = last_tile(act)

                def load_x(s):
                    row = act.value_load(tab[0:1, bass.ds(s + T_ROW, 1)], min_val=0, max_val=PAIRS)
                    rows = act.value_load(tab[0:1, bass.ds(s + T_ROWS, 1)], min_val=0, max_val=T)
                    act.dma_start(x_rows[0:P // 2], xs[l][bass.ds(row, P // 2), :]).then_inc(x_loaded[l], 16)
                    act.dma_start(x_rows[P // 2:P], xs[l][bass.ds(row + P // 2, P // 2), :],
                                  cond=rows > P // 2).then_inc(x_loaded[l], 16)

                def copy_xT(s):
                    act.wait_ge(x_turned[l], s + 1)
                    src = ps[:, B_TURN, :].rearrange("p (k n) -> p k n", n=P)
                    nc.scalar.copy(xT[:, 0:C // 2, :], src).then_inc(xT_act[l], 1)

                def store_y(s, first):
                    row = act.value_load(tab[0:1, bass.ds(s + T_ROW, 1)], min_val=0, max_val=PAIRS)
                    rows = act.value_load(tab[0:1, bass.ds(s + T_ROWS, 1)], min_val=0, max_val=T)
                    act.wait_ge(y_done[l], s + 2)
                    if not first:
                        act.wait_ge(y_stored[l], 32 * s)
                    nc.scalar.copy(y_rows[:, 0:DH], ps[:, B_Y, :]).then_inc(y_act[l], 1)
                    act.wait_ge(y_act[l], s + 1)
                    act.wait_ge(y_dve[l], s + 1)
                    act.dma_start(ys[l][bass.ds(row, P // 2), :], y_rows[0:P // 2]).then_inc(y_stored[l], 16)
                    act.dma_start(ys[l][bass.ds(row + P // 2, P // 2), :], y_rows[P // 2:P],
                                  cond=rows > P // 2).then_inc(y_stored[l], 16)

                def body(s, peeled):
                    act.wait_ge(gu_done[l], s + 1)
                    if not (peeled and s == 0):
                        act.wait_ge(hid_done[l], s)
                    nc.scalar.activation(silu_sb, ps[:, B_GU, 0:F], ACT.Silu).then_inc(silu_done[l], 1)
                    copy_xT(s + 1)
                    load_x(s + 2)
                    if not (peeled and s == 0):
                        store_y(s - 1, peeled)

                act.wait_ge(scattered, 16 * 2 * NT * (l + 1))
                act.wait_ge(pads_stored, 32)
                load_x(0)
                for t in range(2):
                    scale_h(t, h_scaled)
                copy_xT(0)
                load_x(1)
                body(0, True)
                body(1, True)
                with act.Fori(2, last + 1) as s:
                    body(s, False)
                store_y(last, False)
                for t in range(2, NT):
                    scale_h(t, h_scaled)
                act.wait_ge(x_loaded[l], (last + 3) * 32)
                act.wait_ge(y_stored[l], (last + 1) * 32)
                act.sem_inc(ys_complete, 1)

            for t in range(NT):
                copy_hT(t)
            act.wait_ge(rows_turned, 1)
            nc.scalar.copy(cvec[:], ps[:, 0, 0:NV + KB * C])
            nc.scalar.copy(hist_a[:].rearrange("p c n -> p (c n)"), ps[:, 1, 0:C * NS * HA]).then_inc(rows_act, 1)
            for t in range(NT):
                scale_h(t, h_scaled)
            for p in PRODUCTS[0]:
                split_hi(0, p)
                if p.index % 3 != 1:
                    continue
                j = p.index // 3
                act.wait_ge(q_done, 3 * j + 1)
                if j >= 2:
                    act.wait_ge(cv_done, j - 1)
                pair = 2 * ((3 * j) % 4)
                nc.scalar.copy(c_sb[j % 2].rearrange("p (a n) -> p a n", a=2),
                               ps[:, pair:pair + 2, 0:HALF]).then_inc(c_copied, 1)
            state_rows(0, SA)
            act.dma_start(new_a_prompt[0, 0], stage[0:HA, :]).then_inc(state_out, 16)
            act.dma_start(new_a_sample[0].rearrange("s r d -> (s r) d"), stage[HA:SA, :]).then_inc(state_out, 16)
            for layer in L:
                i = 2 * layer
                for t in range(NT + 1):
                    if t < NT:
                        normalise(i * NT + t)
                    if t >= 1:
                        copy_hT((i + 1) * NT + t - 1)
                act.wait_ge(ln_done, (i + 1) * NT)
                load_ln_params(i + 1)
                if layer == 0:
                    act.wait_ge(state_out, 16 * 3)
                    act.dma_start(stage[:], cf_b2[0].partition_broadcast(P)).then_inc(b2_loaded, 16)
                for r in range(2):
                    act.wait_ge(exp_in, 2 * layer + r + 1)
                    if r == 0:
                        nc.scalar.activation(r_g[:, 2], r_g[:, 0], ACT.Exp).then_inc(exp_out, 1)
                    else:
                        nc.scalar.activation(r_small[:, 9], r_small[:, 8], ACT.Exp).then_inc(exp_out, 1)
                experts(layer)
                for t in range(NT + 2):
                    if t < NT:
                        normalise((i + 1) * NT + t)
                    if layer == 0 and t >= 2:
                        copy_hT((i + 2) * NT + t - 2)
                        scale_h(t - 2, h_mul)
                if layer == DEPTH - 1:
                    continue
                act.wait_ge(ln_done, (i + 2) * NT)
                load_ln_params(i + 2)
                def load_history(i):
                    act.dma_start(hb_rows, hb_dram[i * NHB:(i + 1) * NHB, :]).then_inc(hist_loaded, 16)

                def read_history(i):
                    act.wait_ge(hist_turned, i + 1)
                    for b in range(2):
                        last = nc.scalar.copy(mixT[:, 4 * b:4 * b + 4, i * NHB:(i + 1) * NHB],
                                              ps[:, 6 + b, 0:4 * NHB].rearrange("p (j n) -> p j n", n=NHB))
                    last.then_inc(hist_read, 1)

                def sigmoid(j):
                    act.wait_ge(g_done, 2 * j + 1)
                    if j >= 2:
                        act.wait_ge(glu_done, j - 1)
                    pair = 2 * ((2 * j) % 3)
                    nc.scalar.activation(sig[j % 2].rearrange("p (a n) -> p a n", a=2), ps[:, pair:pair + 2, 0:HALF],
                                         ACT.Sigmoid, bias=bias_g(j)).then_inc(sig_done, 1)

                def read_conv(i):
                    j = PE_CONVS[i]
                    act.wait_ge(pe_conv_done, i + 1)
                    nc.scalar.activation(mixT[:, j, :].rearrange("p (a n) -> p a n", a=2), ps[:, 6:8, 0:HALF],
                                         ACT.Identity, bias=conv_b(j)).then_inc(pe_conv_read, 1)

                act.wait_ge(h_scaled, NT * 3)
                load_history(0)
                unread = []
                convs_ended = 0
                for what in PLAN_B:
                    if what[0] == "C":
                        if what[3] == KB:
                            unread.append(convs_ended)
                            convs_ended += 1
                        continue
                    j = what[1]
                    split_hi(1, PRODUCTS[1][2 * j])
                    if j == 1:
                        read_history(1)
                    for i in unread:
                        read_conv(i)
                    unread = []
                    split_hi(1, PRODUCTS[1][2 * j + 1])
                    if j == 0:
                        read_history(0)
                        load_history(1)
                    sigmoid(j)
                for i in unread:
                    read_conv(i)
                state_rows(1, SB)
                act.dma_start(new_b_prompt[0, 0], stage[0:HB, :]).then_inc(state_out, 16)
                act.dma_start(new_b_sample[0, :, HB - DS:HB, :], stage[HB:SB, :]).then_inc(state_out, 16)
                for j in range(C):
                    act.wait_ge(centred, j + 1)
                    if j >= 4:
                        act.wait_ge(squares_used, j - 3)
                    nc.scalar.activation(squares[j % 4], mixT[:, j, :], ACT.Square).then_inc(squared, 1)
                act.wait_ge(vars_done, 1)
                nc.scalar.activation(rstd_sb.rearrange("p (a n) -> p a n", a=2), ps[:, 6:8, 0:HALF], ACT.Sqrt,
                                     bias=eps[:, 0:1], scale=1.0 / D).then_inc(csd_ready, 1)
                for j in range(C):
                    act.wait_ge(normed, j + 1)
                    nc.scalar.activation(mixT[:, j, :], mixT[:, j, :], ACT.Silu, bias=cln_b(j),
                                         scale=cln_g(j)).then_inc(b_mixed, 1)
            act.wait_ge(state_out, 16 * 5)

        @block.gpsimd
        def _(pool):
            done = [0]

            def step(ins):
                done[0] += 1
                ins.then_inc(pool_step, 1)
                pool.wait_ge(pool_step, done[0])

            step(nc.gpsimd.memset(ident[:], 0.0))
            nc.gpsimd.affine_select(out=ident[:], in_=ident[:], compare_op=ALU.not_equal, fill=1.0, base=0,
                                    pattern=[[-1, P]], channel_multiplier=1).then_inc(consts_made, 1)
            step(nc.gpsimd.memset(before16[:], 1.0))
            nc.gpsimd.affine_select(out=before16[:], in_=before16[:], compare_op=ALU.is_gt, fill=0.0, base=0,
                                    pattern=[[1, P]], channel_multiplier=-1).then_inc(consts_made, 1)
            step(nc.gpsimd.memset(valid[:], 1.0))
            nc.gpsimd.affine_select(out=valid[:], in_=valid[:], compare_op=ALU.is_gt, fill=0.0, base=T,
                                    pattern=[[-P, NT]], channel_multiplier=-1).then_inc(consts_made, 1)
            for dst, base, down in ((iota_m[:], -64, 0), (iota_p[:, 0:1], 0, 1), (iota_p[:, 1:2], 0, P)):
                step(nc.gpsimd.iota(dst.bitcast(I32), pattern=[[1, dst.shape[1]]], base=base, channel_multiplier=down))
                nc.gpsimd.tensor_copy(dst, dst.bitcast(I32)).then_inc(iota_made, 1)

            def split_lo(layer, p):
                for c in range(2):
                    i = SPLITS[layer] + 2 * p.index + c
                    pool.wait_ge(w_hi_ready, i + 1)
                    nc.gpsimd.tensor_tensor(w_lo[:, i % 2], raw_chunk(p, c), w_hi[:, i % 2].bitcast(F32),
                                            ALU.subtract).then_inc(w_lo_ready, 1)
                if p.frees:
                    pool.wait_ge(w_lo_ready, i + 1)
                    pool.sem_inc(mixer_slots_used, 1)

            for layer in L:
                if layer == 1:
                    pool.wait_ge(b2_loaded, 16)
                    for t in range(NT):
                        n = ROWS[t]
                        pool.wait_ge(h_mul, t + 1)
                        nc.gpsimd.tensor_tensor(h[0:n, t, :], h[0:n, t, :], stage[0:n, :], ALU.add).then_inc(h_scaled, 1)
                if layer == 0:
                    for p in PRODUCTS[0]:
                        split_lo(0, p)
                else:
                    made = 0
                    for what in PLAN_B:
                        if what[0] == "P":
                            split_lo(1, PRODUCTS[1][2 * what[1]])
                            split_lo(1, PRODUCTS[1][2 * what[1] + 1])
                            continue
                        for k in range(what[2], what[3]):
                            if made >= DIAGS:
                                pool.wait_ge(diag_used, made - DIAGS + 1)
                            nc.gpsimd.tensor_scalar(diag[:, made % DIAGS, :], ident[:], cf_tap(k, what[1]), None,
                                                    ALU.mult).then_inc(diag_ready, 1)
                            made += 1
                pool.wait_ge(pos_ready, layer + 1)
                for t in range(NT):
                    n = ROWS[t]
                    for c in range(2):
                        i = c * NT + t
                        pool.indirect_dma_start(xs[layer][0:PAIRS, :],
                                                bass.IndirectOffsetOnAxis(ap=posi[0:n, i:i + 1], axis=0),
                                                h[0:n, t, :], None).then_inc(scattered, 16)
                pool.wait_ge(ys_complete, layer + 1)
                for t in range(NT):
                    n = ROWS[t]
                    if t >= NB:
                        pool.wait_ge(combined, layer * NT + t - NB + 1)
                    for c in range(2):
                        i = c * NT + t
                        pool.indirect_dma_start(picked[t % NB][0:n, c, :], None, ys[layer][0:PAIRS, :],
                                                bass.IndirectOffsetOnAxis(ap=posi[0:n, i:i + 1], axis=0),
                                                ).then_inc(gathered[t % NB], 16)

        @block.tensor
        def _(pe):
            pe.wait_ge(consts_made, 3)
            pe.wait_ge(zeros_made, 1)
            def turn_h(m):
                t, n = m % NT, ROWS[m % NT]
                if m >= 1:
                    pe.wait_ge(hT_act, m)
                    pe.wait_ge(hT_dve, m)
                for k in range(C):
                    last = nc.tensor.transpose(ps[:, B_TURN + k // 4, (k % 4) * P:(k % 4) * P + n],
                                               h_turn[0:n, t, k, :], ident[0:n, 0:n])
                last.then_inc(h_turned, 1)

            def product_T(layer, p, pair, done):
                for c in range(2):
                    i = SPLITS[layer] + 2 * p.index + c
                    pe.wait_ge(w_hi_ready, i + 1)
                    pe.wait_ge(w_lo_ready, i + 1)
                    for kc in range(KC):
                        k = c * KC + kc
                        for w, x in ((w_hi, hT_hi), (w_hi, hT_lo), (w_lo, hT_hi)):
                            for a in range(2):
                                last = nc.tensor.matmul(ps[:, pair + a, 0:HALF], w[:, i % 2, kc, :],
                                                        x[:, k, a * HALF:(a + 1) * HALF],
                                                        start=(k == 0 and w is w_hi and x is hT_hi),
                                                        stop=(k == C - 1 and w is w_lo))
                    if c == 0:
                        last.then_inc(w_used, 1)
                last.then_inc(done, 1)
                pe.wait_ge(done, p.index + 1)
                pe.sem_inc(w_used, 1)

            def project(layer, t):
                n = ROWS[t]
                n0 = SEQ_MIX[layer] + MIX_SLOTS[layer] - 2
                if t >= 2:
                    pe.wait_ge(z_done, 2 * NT * layer + 2 * (t - 1))
                for half in range(2):
                    w = slot(n0 + half)[:, 0:C * DH].rearrange("p (j n) -> p j n", j=C)
                    pe.wait_ge(weights_ready, n0 + half + 1)
                    for j in range(C):
                        last = nc.tensor.matmul(ps[0:n, 2 * (t % 2) + half, :], mixT[:, j, t * P:t * P + n],
                                                w[:, j, :], start=(j == 0), stop=(j == C - 1))
                    last.then_inc(proj_done, 1)

            def route(layer, t):
                n = ROWS[t]
                m = NT * (2 * layer + 1) + t
                pe.wait_ge(hT_act, m + 1)
                pe.wait_ge(hT_dve, m + 1)
                w = G + E
                for k in range(C):
                    last = nc.tensor.matmul(ps[0:n, B_LOGIT, t * w:(t + 1) * w], xT[:, k, 0:n],
                                            rw[:, layer, k, :], start=(k == 0), stop=(k == C - 1))
                last.then_inc(logits_done, 1)

            def mixer_tail(layer):
                for t in range(NT + 1):
                    if t < NT:
                        project(layer, t)
                    if t == NT - 1:
                        pe.wait_ge(proj_done, 2 * NT * (layer + 1))
                        pe.sem_inc(mixer_slots_used, 2)
                    if t >= 2:
                        route(layer, t - 2)
                    if t >= 1:
                        pe.wait_ge(ln_done, NT * 2 * layer + t)
                        turn_h(NT * (2 * layer + 1) + t - 1)
                route(layer, NT - 1)

            def rank(layer):
                pe.wait_ge(picks_ready, layer + 1)
                for t in range(NT):
                    for u in range(t + 1):
                        nc.tensor.matmul(ps[:, B_RANK, t * E:(t + 1) * E], ones16[:] if u < t else before16[:],
                                         pick16[:, u, :], start=(u == 0), stop=(u == t))
                for u in range(NT):
                    last = nc.tensor.matmul(ps[:, B_RANK, NT * E:(NT + 1) * E], ones16[:], pick16[:, u, :],
                                            start=(u == 0), stop=(u == NT - 1))
                last.then_inc(ranked, 1)
                pe.wait_ge(cols_ready, layer + 1)
                for i in range(6):
                    last = nc.tensor.matmul(ps[0:1, B_LOGIT, i * TAB:(i + 1) * TAB], tcol[:, i:i + 1], ident[:, 0:TAB],
                                            start=True, stop=True)
                last.then_inc(cols_turned, 1)

            def experts(l):
                pe.wait_ge(tab_ready, l + 1)
                last = last_tile(pe)

                def place_of(s):
                    r = pe.value_load(tab[0:1, bass.ds(s + T_RANK, 1)], min_val=0, max_val=E - 1)
                    return r, r % SLOTS

                def turn_x(s):
                    pe.wait_ge(x_loaded[l], (s + 1) * 32)
                    xv = x_rows.rearrange("p (q k) -> p k q", k=C)
                    for k in range(C):
                        last = nc.tensor.transpose(ps[:, B_TURN + k // 4, (k % 4) * P:(k % 4 + 1) * P],
                                                   xv[:, k, :], ident[:])
                        if k == 0 and isinstance(s, int) and s == 0:
                            last.then_inc(y_done[l], 1)
                    last.then_inc(x_turned[l], 1)

                def gate_up(s, peeled):
                    rank, place = place_of(s)
                    pe.wait_ge(xT_act[l], s + 1)
                    pe.wait_ge(xT_dve[l], s + 1)
                    if not (peeled and s == 0):
                        pe.wait_ge(hid_done[l], s)
                    pe.wait_ge(weights_ready, rank + (SEQ_EXP[l] + 1))
                    for k in range(C):
                        last = nc.tensor.matmul(ps[:, B_GU, :], xT[:, k, :], ring_gu[:, bass.ds(place, 1), 0:2, k, :],
                                                start=(k == 0), stop=(k == C - 1))
                    last.then_inc(gu_done[l], 1)

                def down(s, first):
                    rank, place = place_of(s)
                    pe.wait_ge(hidT_ready[l], s + 1)
                    if not first:
                        pe.wait_ge(y_act[l], s)
                        pe.wait_ge(y_dve[l], s)
                    for half in range(2):
                        for k in range(FK):
                            last = nc.tensor.matmul(ps[:, B_Y + half, :], hidT[:, k, :],
                                                    ring_dn[:, bass.ds(place, 1), 2, k, half * DH:(half + 1) * DH],
                                                    start=(k == 0), stop=(k == FK - 1))
                    last.then_inc(y_done[l], 1)

                def turn_hid(s):
                    pe.wait_ge(hid_done[l], s + 1)
                    hv = hid.rearrange("p (q k) -> p k q", k=FK)
                    for k in range(FK):
                        last = nc.tensor.transpose(ps[:, B_HIDT, k * P:(k + 1) * P], hv[:, k, :], ident[:])
                    last.then_inc(hid_turned[l], 1)

                def body(s, peeled):
                    gate_up(s, peeled)
                    turn_x(s + 1)
                    if not (peeled and s == 0):
                        down(s - 1, peeled)
                    turn_hid(s)

                pe.wait_ge(z_done, 2 * NT * (l + 1))
                turn_x(0)
                body(0, True)
                body(1, True)
                with pe.Fori(2, last + 1) as s:
                    body(s, False)
                down(last, False)

            for t in range(NT):
                pe.wait_ge(h_loaded[t], 16 if 0 < t < NT - 1 else 32)
                turn_h(t)
            pe.wait_ge(rows_loaded, 16 * 8)
            nc.tensor.transpose(ps[:, 0, 0:NV], vrows, ident[0:NV, 0:NV])
            for i in range(2):
                nc.tensor.transpose(ps[:, 0, NV + i * KBR:NV + (i + 1) * KBR], cfrows[i], ident[0:KBR, 0:KBR])
            for j in range(C):
                n = NS * HA
                last = nc.tensor.transpose(ps[:, 1, j * n:(j + 1) * n], harows[:, j * P:(j + 1) * P], ident[0:n, 0:n])
            last.then_inc(rows_turned, 1)
            pe.wait_ge(rows_act, 1)
            pe.wait_ge(hT_act, NT)
            pe.wait_ge(hT_dve, NT)
            for p in PRODUCTS[0]:
                j, r = p.index // 3, p.index % 3
                if p.index >= 4:
                    pe.wait_ge((a_mixed, c_copied, cv_done)[r], j - 1 if r == 0 else j)
                product_T(0, p, 2 * (p.index % 4), q_done)
            pe.wait_ge(kept, C)
            for j in range(C):
                last = nc.tensor.transpose(ps[0:SA, 4 + j // 4, (j % 4) * P:(j % 4 + 1) * P], keep[:, j, 0:SA], ident[:])
            last.then_inc(state_turned, 1)
            pe.wait_ge(a_mixed, C)
            mixer_tail(0)
            rank(0)
            experts(0)
            for t in range(NT):
                pe.wait_ge(ln_done, NT + t + 1)
                turn_h(2 * NT + t)
            pe.wait_ge(hT_act, 3 * NT)
            pe.wait_ge(hT_dve, 3 * NT)
            tiles = last_tile(pe) + 1
            pe.wait_ge(y_dve[0], tiles)
            pe.wait_ge(y_act[0], tiles)
            def turn_history(i):
                pe.wait_ge(hist_loaded, 16 * (i + 1))
                if i:
                    pe.wait_ge(hist_read, i)
                for j in range(C):
                    last = nc.tensor.transpose(ps[:, 6 + j // 4, (j % 4) * NHB:(j % 4 + 1) * NHB],
                                               hb_rows[:, j * P:(j + 1) * P], ident[0:NHB, 0:NHB])
                last.then_inc(hist_turned, 1)

            def conv_taps(i, j, k0, k1, used):
                if k0 == 0:
                    pe.wait_ge(glu_done, j + 1)
                    pe.wait_ge(b_step, 2 * j + 2)
                    pe.wait_ge(hist_read, 2)
                    if i:
                        pe.wait_ge(pe_conv_read, i)
                u = glu_of[j]
                for k in range(k0, k1):
                    pe.wait_ge(diag_ready, used + 1)
                    d = diag[:, used % DIAGS, :]
                    ends = dict(start=(k == 0), stop=(k == KB - 1))
                    nc.tensor.matmul(ps[:, 6, 0:HALF], d, u[:, k:k + HALF], **ends)
                    nc.tensor.matmul(ps[:, 7, 0:PH], d, u[:, k + HALF:k + NP], skip_group_check=True, **ends)
                    last = nc.tensor.matmul(seqs(ps[:, 7, PH:HALF], DS), d,
                                            seqs(u[:, WB:LB], HB + DS)[:, :, k:k + DS],
                                            start=False, stop=(k == KB - 1), skip_group_check=True)
                    last.then_inc(diag_used, 1)
                    used += 1
                if k1 == KB:
                    pe.wait_ge(diag_used, used)
                    pe.sem_inc(pe_conv_done, 1)
                return used

            used = convs = 0
            for what in PLAN_B:
                j = what[1]
                if what[0] == "C":
                    used = conv_taps(convs, j, what[2], what[3], used)
                    convs += what[3] == KB
                    continue
                for r in range(2):
                    p = PRODUCTS[1][2 * j + r]
                    if p.index >= 3:
                        pe.wait_ge((glu_done, sig_done)[r], j - 1 if r == 0 else j)
                    product_T(1, p, 2 * (p.index % 3), g_done)
                    if j == 0:
                        turn_history(r)
            pe.wait_ge(pe_conv_read, len(PE_CONVS))
            order = DVE_CONVS[:-2] + list(PE_CONVS) + DVE_CONVS[-2:]
            for j in order:
                if j in DVE_CONVS:
                    pe.wait_ge(conv_done, DVE_CONVS.index(j) + 1)
                for a in range(2):
                    last = nc.tensor.matmul(ps[:, 6 + a, 0:HALF], ones[:], mixT[:, j, a * HALF:(a + 1) * HALF],
                                            start=(j == order[0]), stop=(j == order[-1]))
            last.then_inc(sums_done, 1)
            pe.wait_ge(b_step, 2 * C)
            pe.wait_ge(sig_done, C)
            for j in range(C):
                last = nc.tensor.transpose(ps[0:SB, 4 + j // 4, (j % 4) * P:(j % 4 + 1) * P], keep[:, j, 0:SB], ident[:])
            last.then_inc(state_turned, 1)
            for j in range(C):
                if j == 0:
                    pe.wait_ge(mean_ready, 1)
                pe.wait_ge(squared, j + 1)
                for a in range(2):
                    last = nc.tensor.matmul(ps[:, 6 + a, 0:HALF], ones[:], squares[j % 4][:, a * HALF:(a + 1) * HALF],
                                            start=(j == 0), stop=(j == C - 1))
                last.then_inc(squares_used, 1)
            pe.wait_ge(squares_used, C)
            pe.sem_inc(vars_done, 1)
            pe.wait_ge(b_mixed, C)
            mixer_tail(1)
            rank(1)
            experts(1)

        @block.vector
        def _(dve):
            done = [0]

            def step(ins):
                done[0] += 1
                ins.then_inc(step_s, 1)
                dve.wait_ge(step_s, done[0])

            nc.vector.memset(ones[:], 1.0)
            nc.vector.memset(ones16[:], 1.0)
            nc.vector.memset(eps[:], LN_EPS)
            nc.vector.memset(logit[:], 0.0)
            nc.vector.memset(scan[:], 0.0)
            nc.vector.memset(stage[:], 0.0).then_inc(zeros_made, 1)

            def copy_hT(m):
                t, n = m % NT, ROWS[m % NT]
                if m // NT % 2:
                    dve.wait_ge(h_turned, m + 1)
                    src = ps[:, B_TURN + 1, :].rearrange("p (k n) -> p k n", n=P)[:, :, 0:n]
                    nc.vector.tensor_copy(xT[:, KC:C, 0:n], src).then_inc(hT_dve, 1)
                    return
                dve.wait_ge(hT_act, m + 1)
                for i in range(2):
                    src = ps[:, B_TURN + i, :].rearrange("p (k n) -> p k n", n=P)[:, :, 0:n]
                    at = (slice(None), slice(i * KC, (i + 1) * KC), slice(t * P, t * P + n))
                    last = nc.vector.tensor_tensor(hT_lo[at], src, hT_hi[at].bitcast(F32), ALU.subtract)
                last.then_inc(hT_dve, 1)

            def ln_stats(m):
                t, n = m % NT, ROWS[m % NT]
                for i in range(2):
                    ins = nc.vector.bn_stats(bn[0:n, t, i, :], h[0:n, t, i * DH:(i + 1) * DH])
                step(ins)
                nc.vector.bn_aggr(mv[0:n, t, :], bn[0:n, t].rearrange("p a b -> p (a b)")).then_inc(var_ready, 1)

            def ln_rstd(m):
                t, n = m % NT, ROWS[m % NT]
                dve.wait_ge(sd_ready, m + 1)
                step(nc.vector.reciprocal(sd[0:n, t, 1:2], sd[0:n, t, 0:1]))
                nc.vector.tensor_scalar(sd[0:n, t, 2:3], mv[0:n, t, 0:1], sd[0:n, t, 1:2], -1.0, ALU.mult,
                                        ALU.mult).then_inc(rstd_ready, 1)

            def ln_gain(m):
                t, n = m % NT, ROWS[m % NT]
                dve.wait_ge(ln_applied, m + 1)
                dve.wait_ge(lnp_loaded, 32 * (m // NT + 1))
                nc.vector.tensor_tensor(h[0:n, t, :], h[0:n, t, :], lnp[0:n, 0, :], ALU.mult).then_inc(ln_gained, 1)

            def ln_bias(m):
                t, n = m % NT, ROWS[m % NT]
                dve.wait_ge(ln_gained, m + 1)
                nc.vector.tensor_tensor(h[0:n, t, :], h[0:n, t, :], lnp[0:n, 1, :], ALU.add).then_inc(ln_done, 1)

            def read_logits(layer, t):
                n, w = ROWS[t], G + E
                dve.wait_ge(logits_done, NT * layer + t + 1)
                dve.wait_ge(router_loaded, 16 * 4 * DEPTH)
                nc.vector.tensor_tensor(logit[0:n, t, :], ps[0:n, B_LOGIT, t * w:(t + 1) * w],
                                        rb[0:n, layer, :], ALU.add).then_inc(logits_read, 1)

            def mixer_tail(layer):
                for t in range(NT + 2):
                    m = NT * 2 * layer + t
                    if t < NT:
                        n = ROWS[t]
                        dve.wait_ge(h_scaled, NT * 2 * layer + t + 1)
                        for half in range(2):
                            i = 2 * NT * layer + 2 * t + half
                            dve.wait_ge(proj_done, i + 1)
                            x = h[0:n, t, half * DH:(half + 1) * DH]
                            nc.vector.tensor_tensor(x, ps[0:n, 2 * (t % 2) + half, :], x, ALU.add).then_inc(z_done, 1)
                        dve.wait_ge(z_done, 2 * NT * layer + 2 * t + 2)
                        ln_stats(m)
                        ln_rstd(m)
                    if t >= 2:
                        read_logits(layer, t - 2)
                    if 1 <= t <= NT:
                        copy_hT(NT * (2 * layer + 1) + t - 1)
                    if t < NT:
                        ln_gain(m)
                        ln_bias(m)

            def over(ap, n):
                return ap.unsqueeze(2).to_broadcast([P, NT, n])

            def route(layer):
                dve.wait_ge(logits_read, NT * (layer + 1))
                dve.wait_ge(iota_made, 3)
                dve.wait_ge(consts_made, 3)
                small = [r_small[:, i, :] for i in range(24)]
                gl = logit[:, :, 0:G]
                gmax, gi, gsum, gp, m1, i1, m2, i2, dm, ex, den, w1 = small[0:12]
                assert small[8] is dm and small[9] is ex
                im_g = iota_m[:, 0:G].unsqueeze(1).to_broadcast([P, NT, G])
                im_e = iota_m[:].unsqueeze(1).to_broadcast([P, NT, EG])
                tt = nc.vector.tensor_tensor
                step(nc.vector.tensor_reduce(gmax, gl, AX, ALU.max))
                tt(r_g[:, 0], gl, over(gmax, G), ALU.subtract).then_inc(exp_in, 1)
                step(tt(r_g[:, 1], gl, over(gmax, G), ALU.is_equal))
                step(tt(r_g[:, 1], r_g[:, 1], im_g, ALU.mult))
                step(nc.vector.tensor_reduce(gi, r_g[:, 1], AX, ALU.min))
                step(tt(r_goh[:], im_g, over(gi, G), ALU.is_equal))
                el = logit[:, :, G:G + E].rearrange("p t (g e) -> p t e g", g=G)
                step(tt(r_pick.rearrange("p t (e g) -> p t e g", g=G), el,
                        r_goh[:].unsqueeze(2).to_broadcast([P, NT, EG, G]), ALU.mult))
                sel, q, oh0, sel2, oh1 = [r_e[:, i] for i in range(5)]
                step(nc.vector.tensor_reduce(sel, r_pick.rearrange("p t (e g) -> p t e g", g=G), AX, ALU.add))
                for src, m, i, oh in ((sel, m1, i1, oh0), (sel2, m2, i2, oh1)):
                    step(nc.vector.tensor_reduce(m, src, AX, ALU.max))
                    step(tt(q, src, over(m, EG), ALU.is_equal))
                    step(tt(q, q, im_e, ALU.mult))
                    step(nc.vector.tensor_reduce(i, q, AX, ALU.min))
                    step(tt(oh, im_e, over(i, EG), ALU.is_equal))
                    if src is sel:
                        step(nc.vector.scalar_tensor_tensor(out=sel2, in0=oh, scalar=-3.0e38, in1=sel,
                                                            op0=ALU.mult, op1=ALU.add))
                tt(dm, m2, m1, ALU.subtract).then_inc(exp_in, 1)
                step(tt(r_goh[:], r_goh[:], over(valid[:], G), ALU.mult))
                for c, oh in ((0, oh0), (1, oh1)):
                    ins = tt(pick[:, c].rearrange("p t (g e) -> p t g e", g=G),
                             r_goh[:].unsqueeze(3).to_broadcast([P, NT, G, EG]),
                             oh.unsqueeze(2).to_broadcast([P, NT, G, EG]), ALU.mult)
                step(ins)
                tt(pick16[:], pick[:, 0], pick[:, 1], ALU.add).then_inc(picks_ready, 1)
                dve.wait_ge(exp_out, 2 * layer + 2)
                step(nc.vector.tensor_reduce(gsum, r_g[:, 2], AX, ALU.add))
                step(nc.vector.reciprocal(gp, gsum))
                step(nc.vector.tensor_scalar(den, ex, 1.0, None, ALU.add))
                step(nc.vector.reciprocal(w1, den))
                step(tt(gates[:, 0, :], gp, w1, ALU.mult))
                step(tt(gates[:, 1, :], gates[:, 0, :], ex, ALU.mult))
                dve.wait_ge(ranked, layer + 1)
                H = E // 2
                step(nc.vector.tensor_copy(cnt[:, 0, :], ps[:, B_RANK, NT * E:(NT + 1) * E]))
                step(nc.vector.tensor_scalar(cnt[:, 1, :], cnt[:, 0, :], 0.0, None, ALU.is_gt))
                for i in range(1, NT):
                    step(nc.vector.scalar_tensor_tensor(out=cnt[:, 1, :], in0=cnt[:, 0, :], scalar=float(i * P),
                                                        in1=cnt[:, 1, :], op0=ALU.is_gt, op1=ALU.add))
                nc.vector.memset(cnt[:, 2, 0:EARLY], 1.0)
                nc.vector.tensor_scalar(cnt[:, 2, EARLY:E], cnt[:, 0, EARLY:E], 0.0, None, ALU.is_gt)
                step(nc.vector.tensor_copy(scan[:, 0, 0:2, H:], cnt[:, 0:2]))
                step(nc.vector.tensor_copy(scan[:, 0, 2, H:], cnt[:, 2]))
                src, by = 0, 1
                while by < E:
                    step(tt(scan[:, 1 - src, :, H:], scan[:, src, :, H:], scan[:, src, :, H - by:H + E - by], ALU.add))
                    src, by = 1 - src, 2 * by
                incl = scan[:, src, :, H:]
                step(tt(excl[:], incl, cnt[:], ALU.subtract))
                rankp = ps[:, B_RANK, 0:NT * E].rearrange("p (t e) -> p t e", e=E)
                step(tt(r_pos[:, 0], rankp, excl[:, 0, :].unsqueeze(1).to_broadcast([P, NT, E]), ALU.add))
                for c in range(2):
                    step(tt(r_pos[:, 1], r_pos[:, 0], pick[:, c], ALU.mult))
                    step(nc.vector.tensor_reduce(posf[:, c, :], r_pos[:, 1], AX, ALU.add))
                nc.vector.tensor_copy(posi[:], posf[:].rearrange("p c t -> p (c t)")).then_inc(pos_ready, 1)
                at_p, at_row = iota_p[:, 0:1], iota_p[:, 1:2]
                one = scan[:, 1 - src, 0, H:]
                step(nc.vector.tensor_scalar(one, incl[:, 1, :], at_p, None, ALU.is_le))
                step(nc.vector.scalar_tensor_tensor(out=one, in0=excl[:, 1, :], scalar=at_p, in1=one,
                                                    op0=ALU.is_le, op1=ALU.subtract))
                nc.vector.tensor_copy(tsum[:, 0, :], excl[:, 2, :])
                nc.vector.scalar_tensor_tensor(out=tsum[:, 1, :], in0=excl[:, 1, :], scalar=-float(P),
                                               in1=excl[:, 0, :], op0=ALU.mult, op1=ALU.add)
                nc.vector.scalar_tensor_tensor(out=tsum[:, 2, :], in0=excl[:, 1, :], scalar=float(P),
                                               in1=cnt[:, 0, :], op0=ALU.mult, op1=ALU.add)
                nc.vector.tensor_scalar(tsum[:, 3, :], incl[:, 2, :], at_p, None, ALU.is_le)
                nc.vector.tensor_scalar(tsum[:, 4, :], incl[:, 2, :], at_p, None, ALU.is_le)
                step(nc.vector.scalar_tensor_tensor(out=tsum[:, 5, :], in0=excl[:, 2, :], scalar=at_p,
                                                    in1=cnt[:, 1, :], op0=ALU.is_le, op1=ALU.mult))
                step(tt(tsum[:, 0:3, :], tsum[:, 0:3, :], one.unsqueeze(1).to_broadcast([P, 3, E]), ALU.mult))
                step(nc.vector.tensor_reduce(tcol[:], tsum[:], AX, ALU.add))
                nc.vector.tensor_scalar(tcol[:, 1:2], tcol[:, 1:2], at_row, float(PAIRS), ALU.add, ALU.min)
                nc.vector.tensor_scalar(tcol[:, 2:3], tcol[:, 2:3], at_row, 0.0, ALU.subtract, ALU.max)
                nc.vector.tensor_scalar(tcol[:, 3:4], tcol[:, 3:4], float(E - 1), None, ALU.min).then_inc(cols_ready, 1)
                nc.vector.memset(x_rows[P // 2:P], 0.0)
                if layer > 0:
                    dve.wait_ge(weights_ready, SEQ_MIX[layer] + 2)
                nc.vector.tensor_scalar(tab[:, T_LAST:T_LAST + 1], incl[0:1, 1, E - 1:E], 1.0, None, ALU.subtract)
                dve.wait_ge(cols_turned, layer + 1)
                nc.vector.tensor_copy(tab[:, 0:T_LAST], ps[0:1, B_LOGIT, 0:T_LAST]).then_inc(tab_ready, 1)

            def experts(l):
                dve.wait_ge(tab_ready, l + 1)
                last = last_tile(dve)

                def copy_xT(s):
                    dve.wait_ge(x_turned[l], s + 1)
                    src = ps[:, B_TURN + 1, :].rearrange("p (k n) -> p k n", n=P)
                    nc.vector.tensor_copy(xT[:, C // 2:C, :], src).then_inc(xT_dve[l], 1)

                def copy_y(s, first):
                    dve.wait_ge(y_done[l], s + 2)
                    if not first:
                        dve.wait_ge(y_stored[l], 32 * s)
                    nc.vector.tensor_copy(y_rows[:, DH:D], ps[:, B_Y + 1, :]).then_inc(y_dve[l], 1)

                def body(s, peeled):
                    dve.wait_ge(silu_done[l], s + 1)
                    if not (peeled and s == 0):
                        dve.wait_ge(hid_turned[l], s)
                    nc.vector.tensor_tensor(hid, silu_sb, ps[:, B_GU, F:2 * F], ALU.mult).then_inc(hid_done[l], 1)
                    copy_xT(s + 1)
                    if not (peeled and s == 0):
                        copy_y(s - 1, peeled)
                    dve.wait_ge(hid_turned[l], s + 1)
                    nc.vector.tensor_copy(hidT, ps[:, B_HIDT, 0:F].rearrange("p (k n) -> p k n", n=P)
                                          ).then_inc(hidT_ready[l], 1)

                copy_xT(0)
                body(0, True)
                body(1, True)
                with dve.Fori(2, last + 1) as s:
                    body(s, False)
                copy_y(last, False)

            def combine(layer):
                for t in range(NT):
                    n, b = ROWS[t], t % NB
                    uses = sum(1 for u in range(NT) if u % NB == b) * layer + t // NB + 1
                    dve.wait_ge(gathered[b], 32 * uses)
                    dve.wait_ge(h_scaled, NT * (2 * layer + 1) + t + 1)
                    x = h[0:n, t, :]
                    step(nc.vector.scalar_tensor_tensor(out=x, in0=picked[b][0:n, 0, :], scalar=gates[0:n, 0, t:t + 1],
                                                        in1=x, op0=ALU.mult, op1=ALU.add))
                    nc.vector.scalar_tensor_tensor(out=x, in0=picked[b][0:n, 1, :], scalar=gates[0:n, 1, t:t + 1],
                                                   in1=x, op0=ALU.mult, op1=ALU.add).then_inc(combined, 1)
                    dve.wait_ge(combined, NT * layer + t + 1)
                    m = NT * (2 * layer + 1) + t
                    ln_stats(m)
                    if t >= 1:
                        ln_gain(m - 1)
                    ln_rstd(m)
                    if t >= 1:
                        ln_bias(m - 1)
                    if layer == 0 and t >= 2:
                        copy_hT(2 * NT + t - 2)
                ln_gain(m)
                ln_bias(m)
                if layer == 0:
                    copy_hT(3 * NT - 2)
                    copy_hT(3 * NT - 1)

            for t in range(NT):
                copy_hT(t)
            dve.wait_ge(rows_act, 1)
            for i in range(2):
                step(nc.vector.memset(u_in[i][:, 0:HA], 0.0))
            for j in range(C):
                u, c, pair = u_in[j % 2], c_sb[j % 2], 2 * ((3 * j + 1) % 4)
                nc.vector.tensor_copy(seqs(u[:, WA:LA], HA + DS)[:, :, 0:HA],
                                      hist_a[:, j, :].rearrange("p (s r) -> p s r", r=HA))
                dve.wait_ge(c_copied, j + 1)
                dve.wait_ge(q_done, 3 * j + 2)
                nc.vector.tensor_tensor(u[:, HA:HA + HALF], ps[:, pair, 0:HALF], c[:, 0:HALF], ALU.mult)
                nc.vector.tensor_tensor(u[:, HA + HALF:WA], ps[:, pair + 1, 0:PH], c[:, HALF:NP], ALU.mult)
                ins = nc.vector.tensor_tensor(seqs(u[:, WA:LA], HA + DS)[:, :, HA:HA + DS],
                                              seqs(ps[:, pair + 1, PH:HALF], DS), seqs(c[:, NP:T], DS), ALU.mult)
                ins.then_inc(cv_done, 1)
                dve.wait_ge(cv_done, j + 1)
                nc.vector.tensor_copy(keep[:, j, 0:HA], u[:, NP:WA])
                nc.vector.tensor_copy(keep[:, j, HA:SA].rearrange("p (s r) -> p s r", r=HA),
                                      seqs(u[:, WA:LA], HA + DS)[:, :, DS:DS + HA]).then_inc(kept, 1)
                w = LA - HA
                step(nc.vector.tensor_scalar(acc_a, u[:, 0:w], sc_tap(0, j), None, ALU.mult))
                for k in range(1, KA):
                    step(nc.vector.scalar_tensor_tensor(out=acc_a, in0=u[:, k:k + w], scalar=sc_tap(k, j), in1=acc_a,
                                                        op0=ALU.mult, op1=ALU.add))
                dve.wait_ge(q_done, 3 * j + 3)
                pair = 2 * ((3 * j + 2) % 4)
                m = mixT[:, j, :]
                nc.vector.tensor_tensor(m[:, 0:HALF], ps[:, pair, 0:HALF], acc_a[:, 0:HALF], ALU.mult)
                nc.vector.tensor_tensor(m[:, HALF:NP], ps[:, pair + 1, 0:PH], acc_a[:, HALF:NP], ALU.mult)
                sampled = work[:, 2 * LA + 2 * T + WA:2 * LA + 2 * T + LA]
                ins = nc.vector.tensor_tensor(seqs(m[:, NP:T], DS), seqs(ps[:, pair + 1, PH:HALF], DS),
                                              seqs(sampled, HA + DS)[:, :, 0:DS], ALU.mult)
                ins.then_inc(a_mixed, 1)
            mixer_tail(0)
            route(0)
            experts(0)
            combine(0)
            dve.wait_ge(y_stored[0], (last_tile(dve) + 1) * 32)
            for i in range(4):
                ins = nc.vector.memset(glu[i][:, 0:HB], 0.0)
            ins.then_inc(zeros_made, 1)
            taken = 0

            def gate(j):
                u, sg, pair = glu_of[j], sig[j % 2], 2 * ((2 * j + 1) % 3)
                dve.wait_ge(sig_done, j + 1)
                dve.wait_ge(g_done, 2 * j + 2)
                for out, in0, in1 in (
                        (u[:, HB:HB + HALF], ps[:, pair, 0:HALF], sg[:, 0:HALF]),
                        (u[:, HB + HALF:WB], ps[:, pair + 1, 0:PH], sg[:, HALF:NP]),
                        (seqs(u[:, WB:LB], HB + DS)[:, :, HB:HB + DS], seqs(ps[:, pair + 1, PH:HALF], DS),
                         seqs(sg[:, NP:T], DS))):
                    ins = nc.vector.scalar_tensor_tensor(out=out, in0=in0, scalar=bias_a(j), in1=in1,
                                                         op0=ALU.add, op1=ALU.mult)
                ins.then_inc(glu_done, 1)
                dve.wait_ge(glu_done, j + 1)
                dve.wait_ge(hist_read, 2)
                nc.vector.tensor_copy(seqs(u[:, WB:LB], HB + DS)[:, :, 0:HB],
                                      seqs(mixT[:, j, 0:NS * HB], HB)).then_inc(b_step, 1)
                nc.vector.tensor_copy(keep[:, j, 0:HB], u[:, NP:WB])
                nc.vector.tensor_copy(keep[:, j, HB:SB].rearrange("p (s r) -> p s r", r=DS),
                                      seqs(u[:, WB:LB], HB + DS)[:, :, HB:HB + DS]).then_inc(b_step, 1)
                dve.wait_ge(b_step, 2 * j + 2)

            for j in range(C):
                gate(j)
                if j in PE_CONVS:
                    continue
                u, m = glu_of[j], mixT[:, j, :]
                for k in range(KB):
                    for out, src in ((m[:, 0:NP], u[:, k:k + NP]),
                                     (seqs(m[:, NP:T], DS), seqs(u[:, WB:LB], HB + DS)[:, :, k:k + DS])):
                        if k == 0:
                            ins = nc.vector.tensor_scalar(out, src, cf_tap(k, j), conv_b(j), ALU.mult, ALU.add)
                        else:
                            dve.wait_ge(conv_step, taken - 1)
                            ins = nc.vector.scalar_tensor_tensor(out=out, in0=src, scalar=cf_tap(k, j), in1=out,
                                                                 op0=ALU.mult, op1=ALU.add)
                        ins.then_inc(conv_step, 1)
                        taken += 1
                dve.wait_ge(conv_step, taken)
                dve.sem_inc(conv_done, 1)
            dve.wait_ge(pe_conv_read, len(PE_CONVS))
            dve.wait_ge(sums_done, 1)
            ins = nc.vector.tensor_scalar(mean_sb.rearrange("p (a n) -> p a n", a=2), ps[:, 6:8, 0:HALF], 1.0 / D, None,
                                          ALU.mult)
            ins.then_inc(mean_ready, 1)
            dve.wait_ge(mean_ready, 1)
            for j in range(C):
                nc.vector.tensor_tensor(mixT[:, j, :], mixT[:, j, :], mean_sb, ALU.subtract).then_inc(centred, 1)
            dve.wait_ge(csd_ready, 1)
            step(nc.vector.reciprocal(mean_sb, rstd_sb))
            dve.wait_ge(squared, C)
            for j in range(C):
                nc.vector.tensor_tensor(mixT[:, j, :], mixT[:, j, :], mean_sb, ALU.mult).then_inc(normed, 1)
            mixer_tail(1)
            route(1)
            experts(1)
            combine(1)


_INS = ['x_prompt', 'x_sample', 'state_conv_a', 'state_conv_b', 'meta_tokens', 'sc_w_in', 'sc_conv_w', 'sc_w_out',
        'cf_w_pw1', 'cf_b_pw1', 'cf_conv_w', 'cf_conv_b', 'cf_ln_g', 'cf_ln_b', 'cf_w_pw2', 'cf_b_pw2',
        'ln1_g', 'ln1_b', 'ln2_g', 'ln2_b', 'rt_group_w', 'rt_group_b', 'rt_expert_w', 'rt_expert_b',
        'moe_w_gate', 'moe_w_up', 'moe_w_down']


def kernel(**inputs):
    import numpy as _np
    import concourse.bacc as _bacc
    from concourse import mybir as _mybir
    from concourse.bass_utils import run_bass_kernel_spmd as _run

    nc = _bacc.Bacc("TRN2", target_bir_lowering=False, num_devices=1)
    arrays, args = {}, []
    for name in _INS:
        a = _np.ascontiguousarray(inputs[name])
        arrays[f"in_{name}_dram"] = a
        args.append(nc.dram_tensor(f"in_{name}_dram", a.shape, _mybir.dt.from_np(a.dtype), kind="ExternalInput").ap())
    xp, xsmp = arrays["in_x_prompt_dram"].shape, arrays["in_x_sample_dram"].shape
    sa, sbs = arrays["in_state_conv_a_dram"].shape, arrays["in_state_conv_b_dram"].shape
    outs = [xp, xsmp, (sa[0], xp[0]) + sa[2:], (sbs[0], xp[0]) + sbs[2:], sa, sbs]
    for i, shape in enumerate(outs):
        args.append(nc.dram_tensor(f"out_{i}_dram", shape, _mybir.dt.float32, kind="ExternalOutput").ap())
    build_decoder_step(nc, *args)
    r = _run(nc, [arrays], core_ids=[0])
    return tuple(r.results[0][f"out_{i}_dram"] for i in range(len(outs)))
```

```python
from contextlib import ExitStack

import concourse.bass as bass
from concourse import mybir

ALU = mybir.AluOpType
ACT = mybir.ActivationFunctionType
F32 = mybir.dt.float32
F32R = mybir.dt.float32r
I32 = mybir.dt.int32
U32 = mybir.dt.uint32
BF16 = mybir.dt.bfloat16
AX = mybir.AxisListType.X

P = 128
BANK = 512
ALPHA = 4.0 ** 0.25
LN_EPS = 1e-5


def build_decoder_step(nc, x_prompt, x_sample, state_a, state_b, meta, sc_w_in, sc_conv_w, sc_w_out,
                       cf_w1, cf_b1, cf_conv_w, cf_conv_b, cf_ln_g, cf_ln_b, cf_w2, cf_b2,
                       ln1_g, ln1_b, ln2_g, ln2_b, rg_w, rg_b, re_w, re_b, w_gate, w_up, w_down,
                       y_prompt, y_sample, new_a_prompt, new_b_prompt, new_a_sample, new_b_sample):
    _, SEQ, D = x_prompt.shape
    NS, DS, _ = x_sample.shape
    META = meta.shape[0]
    DEPTH, E, _, F = w_gate.shape
    G = rg_w.shape[2]
    EG = E // G
    KA, KB = sc_conv_w.shape[1], cf_conv_w.shape[1]
    HA, HB = KA - 1, KB - 1
    NP = META + SEQ
    T = NP + NS * DS
    NT = -(-T // P)
    ROWS = [min(P, T - t * P) for t in range(NT)]
    C = D // P
    HALF = T // 2
    PH = NP - HALF
    assert NP > HALF and NP - (NT - 1) * P == META and T % 2 == 0 and HALF <= BANK
    WA = HA + NP
    LA = WA + NS * (HA + DS)
    WB = HB + NP
    LB = WB + NS * (HB + DS)
    SA = HA + NS * HA
    SB = HB + NS * DS
    PAIRS = 2 * T
    XROWS = PAIRS + P
    TILES = (PAIRS - E) // P + E
    TAB = 48
    assert TILES + 4 <= TAB <= P and PAIRS > 2 * P
    T_EXPERT, T_RAW, T_UPTO, T_LAST = (i * TAB for i in range(4, 8))
    PIECES = ((0, P // 4), (P // 4, P // 2), (P // 2, P))
    MOVED = 16 * len(PIECES)
    COLS = 5
    EARLY = 2
    SLOT = 3 * C * F
    SLOTS = 4
    SHARED = SLOTS - 1
    assert E % SLOTS == 0
    WIN_BLOCKS = 2
    PW_BLOCKS = 3
    DH = D // 2

    with ExitStack() as ctx:
        def sb(name, shape, dt=F32):
            return ctx.enter_context(nc.sbuf_tensor(name, shape, dt))

        def sem(name):
            return ctx.enter_context(nc.semaphore(name))

        ps = ctx.enter_context(nc.psum_tensor("ps", [P, 8, BANK], F32))
        B_TURN, B_RANK, B_LOGIT = 6, 4, 5
        B_GU, B_HIDT, B_Y = 0, 1, 2

        DIAGS = 8
        ring = sb("ring", [P, SHARED * SLOT + C * T + DIAGS * P + C * SB])
        assert C * T + DIAGS * P + C * SB >= SLOT
        at = SHARED * SLOT
        mixT = ring[:, at:at + C * T].rearrange("p (c t) -> p c t", c=C)
        at += C * T
        diag = ring[:, at:at + DIAGS * P].rearrange("p (i c) -> p i c", i=DIAGS)
        at += DIAGS * P
        keep = ring[:, at:at + C * SB].rearrange("p (c s) -> p c s", c=C)
        h = sb("h", [P, NT, D])
        hT_hi = sb("hT_hi", [P, C, T], F32R)
        hT_lo = sb("hT_lo", [P, C, T], F32R)
        KC = C // 2
        w_hi = sb("w_hi", [P, 2, KC, P], F32R)
        w_lo = sb("w_lo", [P, 2, KC, P], F32R)
        work = sb("work", [P, 4640])
        stage = sb("stage", [P, D])
        lnp = sb("lnp", [P, 2, D])
        hist_a = sb("hist_a", [P, C, NS * HA])
        NV = KA * C + 2 * C + 3 * C
        cvec = sb("cvec", [P, NV + KB * C])
        rw = sb("rw", [P, DEPTH, C, G + E])
        rb = sb("rb", [P, DEPTH, G + E])
        ones16 = sb("ones16", [P, P], BF16)
        before16 = sb("before16", [P, P], BF16)
        pick16 = sb("pick16", [P, NT, E], BF16)
        ident = sb("ident", [P, P])
        ones = sb("ones", [P, P])
        eps = sb("eps", [P, 1])
        iota_p = sb("iota_p", [P, 2])
        iota_m = sb("iota_m", [P, EG])
        valid = sb("valid", [P, NT])
        logit = sb("logit", [P, NT, G + E])
        r_small = sb("r_small", [P, 24, NT])
        r_g = sb("r_g", [P, 3, NT, G])
        r_goh = sb("r_goh", [P, NT, G])
        pick = sb("pick", [P, 2, NT, E])
        gates = sb("gates", [P, 2, NT])
        posf = sb("posf", [P, 2, NT])
        posi = sb("posi", [P, 2 * NT], U32)
        cnt = sb("cnt", [P, 3, E])
        scan = sb("scan", [P, 2, 3, E // 2 + E])
        excl = sb("excl", [P, 3, E])
        tsum = sb("tsum", [P, COLS + 1, E])
        tcol = sb("tcol", [P, COLS + 2])
        tab = sb("tab", [1, T_LAST + 2], I32)
        bn = sb("bn", [P, NT, 2, 6])
        mv = sb("mv", [P, NT, 2])
        sd = sb("sd", [P, NT, 2])

        u_in = [work[:, i * LA:(i + 1) * LA] for i in range(2)]
        c_sb = [work[:, 2 * LA + i * T:2 * LA + (i + 1) * T] for i in range(2)]
        acc_a = work[:, 2 * LA + 2 * T:2 * LA + 2 * T + LA - HA]
        glu = [work[:, i * LB:(i + 1) * LB] for i in range(4)]
        sig = [work[:, 4 * LB + i * T:4 * LB + (i + 1) * T] for i in range(2)]
        mean_sb, rstd_sb = sig
        squares = [work[:, i * T:(i + 1) * T] for i in range(4)]
        PE_CONVS = (1, 4)
        DVE_CONVS = [j for j in range(C) if j not in PE_CONVS]
        glu_of = {j: glu[i % 2] for i, j in enumerate(DVE_CONVS)} | {j: glu[2 + i] for i, j in enumerate(PE_CONVS)}
        CUT = 20
        PLAN_B = [("P", 0), ("P", 1), ("P", 2), ("P", 3), ("C", 1, 0, CUT), ("P", 4), ("P", 5), ("C", 1, CUT, KB),
                  ("P", 6), ("P", 7), ("C", 4, 0, KB)]
        assert C == 8
        NHB = NS * HB // 2
        hb_rows = stage[0:NHB]
        x_rows = work[:, 0:D]
        xT = work[:, D:2 * D].rearrange("p (k n) -> p k n", n=P)
        y_rows = work[:, 2 * D:3 * D]
        FK = F // P
        parts = [v[:].rearrange("p k t -> p (k t)") for v in (hT_hi, hT_lo)]
        a_hi, a_lo = [v[:, 0:2 * D].rearrange("p (i n) -> p i n", i=2) for v in parts]
        b_hi, b_lo = [v[:, 2 * D:4 * D].rearrange("p (i n) -> p i n", i=2) for v in parts]
        hidT_hi, hidT_lo = [v[:, 4 * D:4 * D + F].rearrange("p (k n) -> p k n", k=FK) for v in parts]
        xT_hi, xT_lo = [v[:].rearrange("p i k c -> p (i k) c") for v in (w_hi, w_lo)]
        assert 4 * D + F <= C * T and C == 8 and FK == 2 and 4 * F == D
        silu_sb = work[:, 3 * D:3 * D + F]
        hid = work[:, 3 * D + F:3 * D + 2 * F]
        picked = [v[:, 2 * D * b:2 * D * (b + 1)].rearrange("p (k d) -> p k d", k=2)
                  for v in (mixT[:].rearrange("p c t -> p (c t)"), work) for b in range(2)]
        NB = len(picked)
        r_e = work[:, 0:6 * NT * EG].rearrange("p (i t e) -> p i t e", t=NT, e=EG)
        r_pick = work[:, 512:512 + NT * E].rearrange("p (t e) -> p t e", e=E)
        r_pos = work[:, 1024:1024 + 2 * NT * E].rearrange("p (i t e) -> p i t e", t=NT, e=E)
        vrows = work[0:NV, 0:P]
        KBR = KB * C // 2
        cfrows = [work[0:KBR, P * (1 + i):P * (2 + i)] for i in range(2)]
        harows = work[0:NS * HA, 3 * P:3 * P + D]

        xs = [nc.dram_tensor(f"x_sorted{l}", (XROWS, D), F32).ap() for l in range(DEPTH)]
        ys = [nc.dram_tensor(f"y_sorted{l}", (XROWS, D), F32).ap() for l in range(DEPTH)]

        def sc_tap(k, j): return cvec[:, k * C + j:k * C + j + 1]
        def bias_a(j): return cvec[:, KA * C + j:KA * C + j + 1]
        def bias_g(j): return cvec[:, KA * C + C + j:KA * C + C + j + 1]
        def conv_b(j): return cvec[:, KA * C + 2 * C + j:KA * C + 2 * C + j + 1]
        def cln_g(j): return cvec[:, KA * C + 3 * C + j:KA * C + 3 * C + j + 1]
        def cln_b(j): return cvec[:, KA * C + 4 * C + j:KA * C + 4 * C + j + 1]
        def cf_tap(k, j): return cvec[:, NV + k * C + j:NV + k * C + j + 1]

        h_turn = h[:].rearrange("p t (q k) -> p t k q", k=C)

        def seqs(ap, width):
            return ap.rearrange("p (s w) -> p s w", w=width)

        h_loaded = [sem(f"h_loaded{t}") for t in range(NT)]
        rows_loaded = sem("rows_loaded")
        router_loaded = sem("router_loaded")
        lnp_loaded = sem("lnp_loaded")
        b2_loaded = sem("b2_loaded")
        pads_stored = sem("pads_stored")
        consts_made = sem("consts_made")
        iota_made = sem("iota_made")
        zeros_made = sem("zeros_made")
        rows_turned = sem("rows_turned")
        rows_act = sem("rows_act")
        w_hi_ready, w_lo_ready, w_used = sem("w_hi_ready"), sem("w_lo_ready"), sem("w_used")
        diag_ready, diag_used = sem("diag_ready"), sem("diag_used")
        pe_conv_done, pe_conv_read = sem("pe_conv_done"), sem("pe_conv_read")
        hist_loaded, hist_turned, hist_read = sem("hist_loaded"), sem("hist_turned"), sem("hist_read")
        squares_used = sem("squares_used")
        slot_loaded = [sem(f"slot_loaded{i}") for i in range(SLOTS)]
        weights_ready = sem("weights_ready")
        mixer_slots_used = sem("mixer_slots_used")
        h_turned = sem("h_turned")
        hT_act, hT_dve = sem("hT_act"), sem("hT_dve")
        q_done = sem("q_done")
        c_copied, cv_done, a_mixed = sem("c_copied"), sem("cv_done"), sem("a_mixed")
        kept = sem("kept")
        g_done = sem("g_done")
        sig_done, glu_done, b_step = sem("sig_done"), sem("glu_done"), sem("b_step")
        conv_step, conv_done = sem("conv_step"), sem("conv_done")
        sums_done, mean_ready, centred, squared = sem("sums_done"), sem("mean_ready"), sem("centred"), sem("squared")
        vars_done, csd_ready, normed, b_mixed = sem("vars_done"), sem("csd_ready"), sem("normed"), sem("b_mixed")
        state_turned, state_act, state_out = sem("state_turned"), sem("state_act"), sem("state_out")
        proj_done, z_done = sem("proj_done"), sem("z_done")
        h_scaled = sem("h_scaled")
        h_mul = sem("h_mul")
        var_ready, sd_ready, rstd_ready = sem("var_ready"), sem("sd_ready"), sem("rstd_ready")
        ln_gained, ln_done = sem("ln_gained"), sem("ln_done")
        logits_done, logits_read = sem("logits_done"), sem("logits_read")
        exp_in, exp_out = sem("exp_in"), sem("exp_out")
        cols_ready, cols_turned = sem("cols_ready"), sem("cols_turned")
        picks_ready, ranked, pos_ready, tab_ready = sem("picks_ready"), sem("ranked"), sem("pos_ready"), sem("tab_ready")
        step_s = sem("dve_step")
        pool_step = sem("pool_step")
        scattered = sem("scattered")
        L = range(DEPTH)
        x_loaded = [sem(f"x_loaded{l}") for l in L]
        x_turned = [sem(f"x_turned{l}") for l in L]
        xT_act = [sem(f"xT_act{l}") for l in L]
        xT_dve = [sem(f"xT_dve{l}") for l in L]
        silu_done = [sem(f"silu_done{l}") for l in L]
        hid_done = [sem(f"hid_done{l}") for l in L]
        hid_turned = [sem(f"hid_turned{l}") for l in L]
        hidT_act = [sem(f"hidT_act{l}") for l in L]
        hidT_ready = [sem(f"hidT_ready{l}") for l in L]
        a_hi_ready, a_lo_ready, a_used = [[sem(f"{n}{l}") for l in L] for n in ("a_hi_ready", "a_lo_ready", "a_used")]
        b_own_hi, b_waits = [[sem(f"{n}{l}") for l in L] for n in ("b_own_hi", "b_waits")]
        b_hi_ready, b_lo_ready, b_used = [[sem(f"{n}{l}") for l in L] for n in ("b_hi_ready", "b_lo_ready", "b_used")]
        y_done = [sem(f"y_done{l}") for l in L]
        y_copied = [sem(f"y_copied{l}") for l in L]
        y_stored = [sem(f"y_stored{l}") for l in L]
        ys_complete = sem("ys_complete")
        gathered = [sem(f"gathered{b}") for b in range(NB)]
        combined = sem("combined")
        out_stored = sem("out_stored")

        NWIN, NWOUT = C // WIN_BLOCKS, 2
        NPW, NPW2 = -(-C // PW_BLOCKS), 2
        MIX_SLOTS = [NWIN + NWOUT, NPW + NPW2]
        SEQ_MIX = [0, MIX_SLOTS[0] + E]
        SEQ_EXP = [MIX_SLOTS[0], MIX_SLOTS[0] + E + MIX_SLOTS[1]]

        MIX_PLACES = [(0, 1, 2, 0, 1, 2), (0, 1, 0, 2, 1)]
        assert [len(v) for v in MIX_PLACES] == MIX_SLOTS

        def place(n):
            layer = 0 if n < SEQ_MIX[1] else 1
            if n >= SEQ_EXP[layer]:
                return (n - SEQ_EXP[layer]) % SLOTS
            return MIX_PLACES[layer][n - SEQ_MIX[layer]]

        def prior(n):
            return max((m for m in range(n) if place(m) == place(n)), default=None)

        class Product:

            def __init__(self, index, n, col, pitch, frees):
                self.index, self.n, self.col, self.pitch, self.frees = index, n, col, pitch, frees

        def products(layer):
            out = []
            for j in range(C):
                per = WIN_BLOCKS if layer == 0 else PW_BLOCKS
                nb = min(per, C - j // per * per)
                groups = 3 if layer == 0 else 2
                for r in range(groups):
                    out.append(Product(groups * j + r, SEQ_MIX[layer] + j // per, (r * nb + j % per) * P,
                                       groups * nb * P, r == groups - 1 and j % per == nb - 1))
            return out

        PRODUCTS = [products(0), products(1)]
        SPLITS = [0, 2 * len(PRODUCTS[0])]

        def raw_chunk(p, c):
            w = slot(p.n)[:, 0:C * p.pitch].rearrange("p (k c) -> p k c", k=C)
            return w[:, c * KC:(c + 1) * KC, p.col:p.col + P]

        LAG = 2

        def slot(n):
            return ring[:, place(n) * SLOT:(place(n) + 1) * SLOT]

        ring_gu = ring[:, 0:SLOTS * SLOT].rearrange("p (s u c k f) -> p s u c k f", s=SLOTS, u=3, c=C // 2, k=2)
        ring_chunks = ring[:, 0:SLOTS * SLOT].rearrange("p (s u q n) -> p s u q n", s=SLOTS, u=3, n=2 * F)

        def gu_chunk(rank, c):
            return ring_gu[:, bass.ds(rank % SLOTS, 1), 0:2, c, :, :]

        def down_chunk(rank, k):
            return ring_chunks[:, bass.ds(rank % SLOTS, 1), 2, 2 * k:2 * k + 2, :]

        def as_gu(ap):
            return ap.rearrange("p (o k u f) -> p o u k f", o=1, u=2, k=2)

        def as_down(ap):
            return ap.rearrange("p (o q n) -> p o q n", o=1, q=2)

        def record(engine, s, n=4):
            return nc.values_load_multi_w_load_instructions(tab[0:1, bass.ds(4 * s + 8, n)], engines=(engine,),
                                                            min_val=0, max_val=4 * PAIRS + 3)[1]

        def rank_of(eng, s):
            return eng.value_load(tab[0:1, bass.ds(4 * s + 4, 1)], min_val=0, max_val=E - 1)

        def last_tile(eng):
            return eng.value_load(tab[0:1, T_LAST:T_LAST + 1], min_val=PAIRS // P - 1, max_val=TILES - 1)

        def tile_before_last(eng):
            return eng.value_load(tab[0:1, T_LAST + 1:T_LAST + 2], min_val=PAIRS // P - 2, max_val=TILES - 2)

        block = ctx.enter_context(nc.Block())

        @block.sync
        def _(sp):
            given = [0] * SLOTS

            def load_mixer(n, pieces):
                for dst, src in pieces:
                    sp.dma_start(dst, src).then_inc(slot_loaded[place(n)], 16)
                    given[place(n)] += 16

            def mixer_pieces(layer, i):
                n = SEQ_MIX[layer] + i
                s = slot(n)
                if layer == 0 and i < NWIN:
                    w = WIN_BLOCKS * P
                    v = s[:, 0:C * 3 * w].rearrange("p (k g c) -> p k g c", k=C, g=3)
                    src = sc_w_in[0].rearrange("(p k) (g c) -> p k g c", k=C, g=3)
                    return [(v[:, :, to, :], src[:, :, g, i * w:(i + 1) * w]) for to, g in ((0, 1), (1, 2), (2, 0))]
                if layer == 1 and i < NPW:
                    nb = min(PW_BLOCKS, C - i * PW_BLOCKS)
                    v = s[:, 0:C * 2 * nb * P].rearrange("p (k g c) -> p k g c", k=C, g=2)
                    src = cf_w1[0].rearrange("(p k) (g c) -> p k g c", k=C, g=2)
                    c0 = i * PW_BLOCKS * P
                    return [(v[:, :, to, :], src[:, :, g, c0:c0 + nb * P]) for to, g in ((0, 1), (1, 0))]
                half = i - (NWIN if layer == 0 else NPW)
                w2 = sc_w_out if layer == 0 else cf_w2
                v = s[:, 0:C * DH].rearrange("p (j n) -> p j n", j=C)
                return [(v, w2[0].rearrange("(j p) n -> p j n", p=P)[:, :, half * DH:(half + 1) * DH])]

            def load_expert(layer, r, number=None):
                s = ring[:, r % SLOTS * SLOT:(r % SLOTS + 1) * SLOT]
                u = C * F
                if number is None:
                    e, cond = r, {}
                else:
                    e = sp.value_load(tab[0:1, bass.ds(number + T_EXPERT, 1)], min_val=0, max_val=E - 1)
                    raw = sp.value_load(tab[0:1, bass.ds(number + T_RAW, 1)], min_val=0, max_val=E)
                    cond = dict(cond=raw < E)
                e1 = bass.ds(e, 1)
                for dst, src in ((s[:, 0:u], w_gate[layer, e1].rearrange("e (p k) f -> p (e k f)", k=C)),
                                 (s[:, u:2 * u], w_up[layer, e1].rearrange("e (p k) f -> p (e k f)", k=C)),
                                 (s[:, 2 * u:3 * u], w_down[layer, e1].rearrange("e (p k) d -> p (e k d)", k=FK))):
                    sp.dma_start(dst, src, **cond).then_inc(slot_loaded[r % SLOTS], 16)

            def pass_on(n):
                sp.wait_ge(slot_loaded[place(n)], given[place(n)])
                sp.sem_inc(weights_ready, 1)

            for layer in L:
                if layer > 0:
                    sp.wait_ge(tab_ready, layer)
                for i in range(MIX_SLOTS[layer] + SLOTS):
                    n = SEQ_MIX[layer] + i
                    if n >= LAG:
                        pass_on(n - LAG)
                    m = prior(n)
                    if i == MIX_SLOTS[layer] + EARLY:
                        sp.wait_ge(tab_ready, layer + 1)
                        sp.wait_ge(x_loaded[layer], MOVED)
                    if m is not None and place(n) != SHARED:
                        if layer > 0 and m < SEQ_MIX[layer]:
                            at = T_UPTO + m - SEQ_EXP[layer - 1]
                            upto = sp.value_load(tab[0:1, at:at + 1], min_val=0, max_val=TILES)
                            sp.wait_ge(y_done[layer - 1], upto + 1)
                        else:
                            used = sum(MIX_SLOTS[:layer]) + m - SEQ_MIX[layer] + 1
                            sp.wait_ge(mixer_slots_used, used)
                    if n == 1:
                        for t in range(NT):
                            sp.wait_ge(h_loaded[t], 16 if 0 < t < NT - 1 else 32)
                        sp.wait_ge(rows_loaded, 16 * 8)
                    if i < MIX_SLOTS[layer]:
                        load_mixer(n, mixer_pieces(layer, i))
                    else:
                        rank = i - MIX_SLOTS[layer]
                        load_expert(layer, rank, rank if rank >= EARLY else None)
                        given[place(n)] += 48
                base = list(given)
                with sp.Fori(1, E // SLOTS) as g:
                    for r in range(SLOTS):
                        behind = (r - LAG) % SLOTS
                        sofar = g * 48 - 48 + base[behind] if r < LAG else g * 48 + base[behind]
                        sp.wait_ge(slot_loaded[behind], sofar)
                        sp.sem_inc(weights_ready, 1)
                        upto = sp.value_load(tab[0:1, bass.ds(g * SLOTS + (T_UPTO + r - SLOTS), 1)],
                                             min_val=0, max_val=TILES)
                        sp.wait_ge(y_done[layer], upto + 1)
                        load_expert(layer, r, g * SLOTS + r)
                for r in range(SLOTS):
                    given[r] = base[r] + 48 * (E // SLOTS - 1)
            for i in range(LAG):
                pass_on(SEQ_EXP[-1] + E - LAG + i)

            for t in range(NT):
                sp.wait_ge(ln_done, NT * (2 * DEPTH - 1) + t + 1)
                lo = META if t == 0 else 0
                hi = META if t == NT - 1 else ROWS[t]
                r0 = t * P + lo - META
                sp.dma_start(y_prompt[0, r0:r0 + hi - lo, :], h[lo:hi, t, :]).then_inc(out_stored, 16)
                if t == NT - 1:
                    sp.dma_start(y_sample.rearrange("s t d -> (s t) d"), h[META:ROWS[t], t, :]).then_inc(out_stored, 16)
            sp.wait_ge(out_stored, 16 * (NT + 1))

        @block.scalar
        def _(act):
            act.dma_start(h[0:META, 0, :], meta).then_inc(h_loaded[0], 16)
            act.dma_start(h[META:P, 0, :], x_prompt[0, 0:P - META, :]).then_inc(h_loaded[0], 16)
            for t in range(1, NT - 1):
                act.dma_start(h[:, t, :], x_prompt[0, t * P - META:(t + 1) * P - META, :]).then_inc(h_loaded[t], 16)
            act.dma_start(h[0:META, NT - 1, :], x_prompt[0, SEQ - META:SEQ, :]).then_inc(h_loaded[NT - 1], 16)
            act.dma_start(h[META:META + NS * DS, NT - 1, :],
                          x_sample.rearrange("s t d -> (s t) d")).then_inc(h_loaded[NT - 1], 16)
            at = 0
            for v in (sc_conv_w[0].rearrange("k (j c) -> (k j) c", c=P),
                      cf_b1[0:1].rearrange("o (j c) -> (o j) c", c=P),
                      cf_conv_b[0:1].rearrange("o (j c) -> (o j) c", c=P),
                      cf_ln_g[0:1].rearrange("o (j c) -> (o j) c", c=P),
                      cf_ln_b[0:1].rearrange("o (j c) -> (o j) c", c=P)):
                n = v.shape[0]
                act.dma_start(vrows[at:at + n, :], v).then_inc(rows_loaded, 16)
                at += n
            taps = cf_conv_w[0].rearrange("k (j c) -> (k j) c", c=P)
            hb_dram = state_b[0].rearrange("s r d -> (s r) d")
            for i in range(2):
                act.dma_start(cfrows[i], taps[i * KBR:(i + 1) * KBR, :]).then_inc(rows_loaded, 16)
            act.dma_start(harows, state_a[0].rearrange("s r d -> (s r) d")).then_inc(rows_loaded, 16)
            for l in L:
                act.dma_start(rw[:, l, :, 0:G], rg_w[l].rearrange("(p k) g -> p k g", k=C)).then_inc(router_loaded, 16)
                act.dma_start(rw[:, l, :, G:G + E], re_w[l].rearrange("(p k) e -> p k e", k=C)).then_inc(router_loaded, 16)
                act.dma_start(rb[:, l, 0:G], rg_b[l].partition_broadcast(P)).then_inc(router_loaded, 16)
                act.dma_start(rb[:, l, G:G + E], re_b[l].partition_broadcast(P)).then_inc(router_loaded, 16)
            act.dma_start(new_b_sample[0, :, 0:HB - DS, :], state_b[0, :, DS:HB, :]).then_inc(state_out, 16)

            def load_ln_params(i):
                gp, bp = ((ln1_g, ln1_b), (ln2_g, ln2_b))[i % 2]
                act.dma_start(lnp[:, 0, :], gp[i // 2].partition_broadcast(P)).then_inc(lnp_loaded, 16)
                act.dma_start(lnp[:, 1, :], bp[i // 2].partition_broadcast(P)).then_inc(lnp_loaded, 16)

            load_ln_params(0)
            act.wait_ge(zeros_made, 1)
            for l in L:
                act.dma_start(xs[l][PAIRS:XROWS, :], stage[:]).then_inc(pads_stored, 16)

            def copy_hT(m):
                t, n = m % NT, ROWS[m % NT]
                act.wait_ge(h_turned, m + 1)
                for i in range(1 if m // NT % 2 else 2):
                    src = ps[:, B_TURN + i, :].rearrange("p (k n) -> p k n", n=P)[:, :, 0:n]
                    if m // NT % 2:
                        last = nc.scalar.copy(xT[:, 0:KC, 0:n], src)
                    else:
                        last = nc.scalar.copy(hT_hi[:, i * KC:(i + 1) * KC, t * P:t * P + n], src)
                last.then_inc(hT_act, 1)

            def split_hi(layer, p):
                act.wait_ge(weights_ready, p.n + 1)
                for c in range(2):
                    i = SPLITS[layer] + 2 * p.index + c
                    if i >= 2:
                        act.wait_ge(w_used, i - 1)
                    nc.scalar.copy(w_hi[:, i % 2], raw_chunk(p, c)).then_inc(w_hi_ready, 1)

            def scale_h(t, signal):
                nc.scalar.mul(h[0:ROWS[t], t, :], h[0:ROWS[t], t, :], ALPHA).then_inc(signal, 1)

            def deviation(m):
                t, n = m % NT, ROWS[m % NT]
                act.wait_ge(var_ready, m + 1)
                nc.scalar.activation(sd[0:n, t, 0:1], mv[0:n, t, 1:2], ACT.Sqrt, bias=eps[0:n, 0:1]).then_inc(sd_ready, 1)

            def state_rows(layer, n):
                act.wait_ge(state_turned, layer + 1)
                if layer == 0:
                    act.wait_ge(pads_stored, 32)
                else:
                    act.wait_ge(hist_turned, 2)
                for i in range(2):
                    last = nc.scalar.copy(stage[0:n, i * DH:(i + 1) * DH], ps[0:n, 4 + i, :])
                last.then_inc(state_act, 1)
                act.wait_ge(state_act, layer + 1)

            def experts(l):
                act.wait_ge(tab_ready, l + 1)
                last, before_last = last_tile(act), tile_before_last(act)

                def move(place, signal, pieces):
                    for i, (dst, src) in enumerate(pieces):
                        act.dma_start(dst, src, **(dict(cond=place % 4 > i - 1) if i else {})).then_inc(signal, 16)

                def load_x(place):
                    row = place // 4
                    move(place, x_loaded[l], [(x_rows[a:b], xs[l][bass.ds(row + a, b - a), :]) for a, b in PIECES])

                def copy_xT(s):
                    act.wait_ge(x_turned[l], s + 1)
                    nc.scalar.copy(xT_hi.rearrange("p (b k) n -> p b (k n)", b=2),
                                   ps[:, B_TURN:B_TURN + 2, :]).then_inc(xT_act[l], 1)

                def hi(buffer, chunk):
                    view = as_gu if len(chunk.shape) == 5 else as_down
                    nc.scalar.copy(view(buffer), chunk).then_inc(a_hi_ready[l], 1)

                def store_y(done, place):
                    row = place // 4
                    act.wait_ge(y_copied[l], done)
                    move(place, y_stored[l], [(ys[l][bass.ds(row + a, b - a), :], y_rows[a:b]) for a, b in PIECES])

                def body(s, before, first=False, ends=False):
                    rank, rank_before, place_y, place_x = record(mybir.EngineType.Activation, s)
                    if before is not None:
                        for k in range(FK):
                            act.wait_ge(a_used[l], 3 * s + k)
                            hi(a_hi[:, k], down_chunk(rank_before, k))
                    act.wait_ge(b_used[l], 2 * s + 2)
                    if before is not None:
                        act.wait_ge(hid_done[l], s)
                    nc.scalar.activation(silu_sb, ps[:, B_GU, 0:F], ACT.Silu).then_inc(silu_done[l], 1)
                    copy_xT(s + 1)
                    if not ends:
                        act.wait_ge(weights_ready, rank + (SEQ_EXP[l] + 1))
                        nc.scalar.copy(as_gu(b_hi[:, 1]), gu_chunk(rank, 3)).then_inc(b_hi_ready[l], 1)
                    if before is not None and not first:
                        store_y(before, place_y)
                    if not ends:
                        for i in range(2):
                            if before is not None and i == 1:
                                act.wait_ge(y_done[l], s + 1)
                            else:
                                act.wait_ge(a_used[l], i + 1 if before is None else 3 * s + 2)
                            hi(a_hi[:, i], gu_chunk(rank, 1 + i))
                    load_x(place_x)
                    act.wait_ge(hid_turned[l], s + 1)
                    nc.scalar.copy(hidT_hi, ps[:, B_HIDT, 0:F].rearrange("p (k n) -> p k n", k=FK)).then_inc(hidT_act[l], 1)

                act.wait_ge(scattered, 16 * 2 * NT * (l + 1))
                act.wait_ge(pads_stored, 32)
                rank, *_, place_x = record(mybir.EngineType.Activation, -1)
                load_x(act.value_load(tab[0:1, 3:4], min_val=0, max_val=4 * PAIRS + 3))
                act.wait_ge(weights_ready, rank + (SEQ_EXP[l] + 1))
                nc.scalar.copy(as_gu(b_hi[:, 1]), gu_chunk(rank, 3)).then_inc(b_hi_ready[l], 1)
                for i in range(2):
                    hi(a_hi[:, i], gu_chunk(rank, 1 + i))
                copy_xT(0)
                load_x(place_x)
                for t in range(2):
                    scale_h(t, h_scaled)
                body(0, None)
                body(1, 0, first=True)
                with act.Fori(2, last) as s:
                    body(s, s - 1)
                body(last, before_last, ends=True)
                _, rank, place, _ = record(mybir.EngineType.Activation, last + 1)
                place_last = record(mybir.EngineType.Activation, last + 2)[2]
                store_y(last, place)
                for k in range(FK):
                    if k == 0:
                        act.wait_ge(a_used[l], 3 * last + 2)
                    else:
                        act.wait_ge(y_done[l], last + 1)
                    hi(a_hi[:, k], down_chunk(rank, k))
                store_y(last + 1, place_last)
                for t in range(2, NT):
                    scale_h(t, h_scaled)
                act.wait_ge(x_loaded[l], (last + 3) * MOVED)
                act.wait_ge(y_stored[l], (last + 1) * MOVED)
                act.sem_inc(ys_complete, 1)

            for t in range(NT):
                copy_hT(t)
            act.wait_ge(rows_turned, 1)
            nc.scalar.copy(cvec[:], ps[:, 0, 0:NV + KB * C])
            nc.scalar.copy(hist_a[:].rearrange("p c n -> p (c n)"), ps[:, 1, 0:C * NS * HA]).then_inc(rows_act, 1)
            for t in range(NT):
                scale_h(t, h_scaled)
            for p in PRODUCTS[0]:
                split_hi(0, p)
                if p.index % 3 != 1:
                    continue
                j = p.index // 3
                act.wait_ge(q_done, 3 * j + 1)
                if j >= 2:
                    act.wait_ge(cv_done, j - 1)
                pair = 2 * ((3 * j) % 4)
                nc.scalar.copy(c_sb[j % 2].rearrange("p (a n) -> p a n", a=2),
                               ps[:, pair:pair + 2, 0:HALF]).then_inc(c_copied, 1)
            state_rows(0, SA)
            act.dma_start(new_a_prompt[0, 0], stage[0:HA, :]).then_inc(state_out, 16)
            act.dma_start(new_a_sample[0].rearrange("s r d -> (s r) d"), stage[HA:SA, :]).then_inc(state_out, 16)
            for layer in L:
                i = 2 * layer
                for t in range(NT + 1):
                    if t < NT:
                        deviation(i * NT + t)
                    if t >= 1:
                        copy_hT((i + 1) * NT + t - 1)
                act.wait_ge(ln_done, (i + 1) * NT)
                load_ln_params(i + 1)
                if layer == 0:
                    act.wait_ge(state_out, 16 * 3)
                    act.dma_start(stage[:], cf_b2[0].partition_broadcast(P)).then_inc(b2_loaded, 16)
                for r in range(2):
                    act.wait_ge(exp_in, 2 * layer + r + 1)
                    if r == 0:
                        nc.scalar.activation(r_g[:, 2], r_g[:, 0], ACT.Exp).then_inc(exp_out, 1)
                    else:
                        nc.scalar.activation(r_small[:, 9], r_small[:, 8], ACT.Exp).then_inc(exp_out, 1)
                experts(layer)
                for t in range(NT + 1):
                    if t < NT:
                        deviation((i + 1) * NT + t)
                    if layer == 0 and t >= 1:
                        copy_hT((i + 2) * NT + t - 1)
                        scale_h(t - 1, h_mul)
                if layer == DEPTH - 1:
                    continue
                act.wait_ge(ln_done, (i + 2) * NT)
                load_ln_params(i + 2)
                def load_history(i):
                    act.dma_start(hb_rows, hb_dram[i * NHB:(i + 1) * NHB, :]).then_inc(hist_loaded, 16)

                def read_history(i):
                    act.wait_ge(hist_turned, i + 1)
                    for b in range(2):
                        last = nc.scalar.copy(mixT[:, 4 * b:4 * b + 4, i * NHB:(i + 1) * NHB],
                                              ps[:, 6 + b, 0:4 * NHB].rearrange("p (j n) -> p j n", n=NHB))
                    last.then_inc(hist_read, 1)

                def sigmoid(j):
                    act.wait_ge(g_done, 2 * j + 1)
                    if j >= 2:
                        act.wait_ge(glu_done, j - 1)
                    pair = 2 * ((2 * j) % 3)
                    nc.scalar.activation(sig[j % 2].rearrange("p (a n) -> p a n", a=2), ps[:, pair:pair + 2, 0:HALF],
                                         ACT.Sigmoid, bias=bias_g(j)).then_inc(sig_done, 1)

                def read_conv(i):
                    j = PE_CONVS[i]
                    act.wait_ge(pe_conv_done, i + 1)
                    nc.scalar.activation(mixT[:, j, :].rearrange("p (a n) -> p a n", a=2), ps[:, 6:8, 0:HALF],
                                         ACT.Identity, bias=conv_b(j)).then_inc(pe_conv_read, 1)

                act.wait_ge(h_scaled, NT * 3)
                load_history(0)
                unread = []
                convs_ended = 0
                for what in PLAN_B:
                    if what[0] == "C":
                        if what[3] == KB:
                            unread.append(convs_ended)
                            convs_ended += 1
                        continue
                    j = what[1]
                    split_hi(1, PRODUCTS[1][2 * j])
                    if j == 1:
                        read_history(1)
                    for i in unread:
                        read_conv(i)
                    unread = []
                    split_hi(1, PRODUCTS[1][2 * j + 1])
                    if j == 0:
                        read_history(0)
                        load_history(1)
                    sigmoid(j)
                for i in unread:
                    read_conv(i)
                state_rows(1, SB)
                act.dma_start(new_b_prompt[0, 0], stage[0:HB, :]).then_inc(state_out, 16)
                act.dma_start(new_b_sample[0, :, HB - DS:HB, :], stage[HB:SB, :]).then_inc(state_out, 16)
                for j in range(C):
                    act.wait_ge(centred, j + 1)
                    if j >= 4:
                        act.wait_ge(squares_used, j - 3)
                    nc.scalar.activation(squares[j % 4], mixT[:, j, :], ACT.Square).then_inc(squared, 1)
                act.wait_ge(vars_done, 1)
                nc.scalar.activation(rstd_sb.rearrange("p (a n) -> p a n", a=2), ps[:, 6:8, 0:HALF], ACT.Sqrt,
                                     bias=eps[:, 0:1], scale=1.0 / D).then_inc(csd_ready, 1)
                for j in range(C):
                    act.wait_ge(normed, j + 1)
                    nc.scalar.activation(mixT[:, j, :], mixT[:, j, :], ACT.Silu, bias=cln_b(j),
                                         scale=cln_g(j)).then_inc(b_mixed, 1)
            act.wait_ge(state_out, 16 * 5)

        @block.gpsimd
        def _(pool):
            done = [0]

            def step(ins):
                done[0] += 1
                ins.then_inc(pool_step, 1)
                pool.wait_ge(pool_step, done[0])

            step(nc.gpsimd.memset(ident[:], 0.0))
            nc.gpsimd.affine_select(out=ident[:], in_=ident[:], compare_op=ALU.not_equal, fill=1.0, base=0,
                                    pattern=[[-1, P]], channel_multiplier=1).then_inc(consts_made, 1)
            step(nc.gpsimd.memset(before16[:], 1.0))
            nc.gpsimd.affine_select(out=before16[:], in_=before16[:], compare_op=ALU.is_gt, fill=0.0, base=0,
                                    pattern=[[1, P]], channel_multiplier=-1).then_inc(consts_made, 1)
            step(nc.gpsimd.memset(valid[:], 1.0))
            nc.gpsimd.affine_select(out=valid[:], in_=valid[:], compare_op=ALU.is_gt, fill=0.0, base=T,
                                    pattern=[[-P, NT]], channel_multiplier=-1).then_inc(consts_made, 1)
            for dst, base, down in ((iota_m[:], -64, 0), (iota_p[:, 0:1], 0, 1), (iota_p[:, 1:2], 0, P)):
                step(nc.gpsimd.iota(dst.bitcast(I32), pattern=[[1, dst.shape[1]]], base=base, channel_multiplier=down))
                nc.gpsimd.tensor_copy(dst, dst.bitcast(I32)).then_inc(iota_made, 1)

            def split_lo(layer, p):
                for c in range(2):
                    i = SPLITS[layer] + 2 * p.index + c
                    pool.wait_ge(w_hi_ready, i + 1)
                    nc.gpsimd.tensor_tensor(w_lo[:, i % 2], raw_chunk(p, c), w_hi[:, i % 2].bitcast(F32),
                                            ALU.subtract).then_inc(w_lo_ready, 1)
                if p.frees:
                    pool.wait_ge(w_lo_ready, i + 1)
                    pool.sem_inc(mixer_slots_used, 1)

            for layer in L:
                if layer == 1:
                    pool.wait_ge(b2_loaded, 16)
                    for t in range(NT):
                        n = ROWS[t]
                        pool.wait_ge(h_mul, t + 1)
                        nc.gpsimd.tensor_tensor(h[0:n, t, :], h[0:n, t, :], stage[0:n, :], ALU.add).then_inc(h_scaled, 1)
                if layer == 0:
                    for p in PRODUCTS[0]:
                        split_lo(0, p)
                else:
                    made = 0
                    for what in PLAN_B:
                        if what[0] == "P":
                            split_lo(1, PRODUCTS[1][2 * what[1]])
                            split_lo(1, PRODUCTS[1][2 * what[1] + 1])
                            continue
                        for k in range(what[2], what[3]):
                            if made >= DIAGS:
                                pool.wait_ge(diag_used, made - DIAGS + 1)
                            nc.gpsimd.tensor_scalar(diag[:, made % DIAGS, :], ident[:], cf_tap(k, what[1]), None,
                                                    ALU.mult).then_inc(diag_ready, 1)
                            made += 1
                pool.wait_ge(pos_ready, layer + 1)
                for t in range(NT):
                    n = ROWS[t]
                    for c in range(2):
                        i = c * NT + t
                        pool.indirect_dma_start(xs[layer][0:PAIRS, :],
                                                bass.IndirectOffsetOnAxis(ap=posi[0:n, i:i + 1], axis=0),
                                                h[0:n, t, :], None).then_inc(scattered, 16)
                pool.wait_ge(tab_ready, layer + 1)
                last = last_tile(pool)

                def seen(semaphore, value):
                    pool.wait_ge(semaphore, value)
                    pool.sem_inc(b_waits[layer], 1)

                def split_pair(s, first):
                    rank = rank_of(pool, s)
                    seen(weights_ready, rank + (SEQ_EXP[layer] + 1))
                    if not first:
                        seen(b_used[layer], 2 * s - 1)
                    nc.gpsimd.tensor_copy(as_gu(b_hi[:, 0]), gu_chunk(rank, 0)).then_inc(b_own_hi[layer], 1)
                    for i, ready in enumerate((b_own_hi, b_hi_ready)):
                        seen(ready[layer], s + 1)
                        nc.gpsimd.tensor_tensor(as_gu(b_lo[:, i]), gu_chunk(rank, 3 * i), as_gu(b_hi[:, i]).bitcast(F32),
                                                ALU.subtract).then_inc(b_lo_ready[layer], 1)

                split_pair(0, True)
                with pool.Fori(1, last + 1) as s:
                    split_pair(s, False)
                pool.wait_ge(ys_complete, layer + 1)
                for t in range(NT):
                    n = ROWS[t]
                    if t >= NB:
                        pool.wait_ge(combined, layer * NT + t - NB + 1)
                    for c in range(2):
                        i = c * NT + t
                        pool.indirect_dma_start(picked[t % NB][0:n, c, :], None, ys[layer][0:PAIRS, :],
                                                bass.IndirectOffsetOnAxis(ap=posi[0:n, i:i + 1], axis=0),
                                                ).then_inc(gathered[t % NB], 16)

        @block.tensor
        def _(pe):
            pe.wait_ge(consts_made, 3)
            pe.wait_ge(zeros_made, 1)
            def turn_h(m):
                t, n = m % NT, ROWS[m % NT]
                if m >= 1:
                    pe.wait_ge(hT_act, m)
                    pe.wait_ge(hT_dve, m)
                for k in range(C):
                    last = nc.tensor.transpose(ps[:, B_TURN + k // 4, (k % 4) * P:(k % 4) * P + n],
                                               h_turn[0:n, t, k, :], ident[0:n, 0:n])
                last.then_inc(h_turned, 1)

            def product_T(layer, p, pair, done):
                for c in range(2):
                    i = SPLITS[layer] + 2 * p.index + c
                    pe.wait_ge(w_hi_ready, i + 1)
                    pe.wait_ge(w_lo_ready, i + 1)
                    for kc in range(KC):
                        k = c * KC + kc
                        for w, x in ((w_hi, hT_hi), (w_hi, hT_lo), (w_lo, hT_hi)):
                            for a in range(2):
                                last = nc.tensor.matmul(ps[:, pair + a, 0:HALF], w[:, i % 2, kc, :],
                                                        x[:, k, a * HALF:(a + 1) * HALF],
                                                        start=(k == 0 and w is w_hi and x is hT_hi),
                                                        stop=(k == C - 1 and w is w_lo))
                    if c == 0:
                        last.then_inc(w_used, 1)
                last.then_inc(done, 1)
                pe.wait_ge(done, p.index + 1)
                pe.sem_inc(w_used, 1)

            def project(layer, t):
                n = ROWS[t]
                n0 = SEQ_MIX[layer] + MIX_SLOTS[layer] - 2
                if t >= 2:
                    pe.wait_ge(z_done, 2 * NT * layer + 2 * (t - 1))
                for half in range(2):
                    w = slot(n0 + half)[:, 0:C * DH].rearrange("p (j n) -> p j n", j=C)
                    pe.wait_ge(weights_ready, n0 + half + 1)
                    for j in range(C):
                        last = nc.tensor.matmul(ps[0:n, 2 * (t % 2) + half, :], mixT[:, j, t * P:t * P + n],
                                                w[:, j, :], start=(j == 0), stop=(j == C - 1))
                    last.then_inc(proj_done, 1)

            def route(layer, t):
                n = ROWS[t]
                m = NT * (2 * layer + 1) + t
                pe.wait_ge(hT_act, m + 1)
                pe.wait_ge(hT_dve, m + 1)
                w = G + E
                for k in range(C):
                    last = nc.tensor.matmul(ps[0:n, B_LOGIT, t * w:(t + 1) * w], xT[:, k, 0:n],
                                            rw[:, layer, k, :], start=(k == 0), stop=(k == C - 1))
                last.then_inc(logits_done, 1)

            def mixer_tail(layer):
                for t in range(NT + 1):
                    if t < NT:
                        project(layer, t)
                    if t == NT - 1:
                        pe.wait_ge(proj_done, 2 * NT * (layer + 1))
                        pe.sem_inc(mixer_slots_used, 2)
                    if t >= 2:
                        route(layer, t - 2)
                    if t >= 1:
                        pe.wait_ge(ln_done, NT * 2 * layer + t)
                        turn_h(NT * (2 * layer + 1) + t - 1)
                route(layer, NT - 1)

            def rank(layer):
                pe.wait_ge(picks_ready, layer + 1)
                for t in range(NT):
                    for u in range(t + 1):
                        nc.tensor.matmul(ps[:, B_RANK, t * E:(t + 1) * E], ones16[:] if u < t else before16[:],
                                         pick16[:, u, :], start=(u == 0), stop=(u == t))
                for u in range(NT):
                    last = nc.tensor.matmul(ps[:, B_RANK, NT * E:(NT + 1) * E], ones16[:], pick16[:, u, :],
                                            start=(u == 0), stop=(u == NT - 1))
                last.then_inc(ranked, 1)
                pe.wait_ge(cols_ready, layer + 1)
                for i in range(COLS):
                    last = nc.tensor.matmul(ps[0:1, B_LOGIT, i * TAB:(i + 1) * TAB], tcol[:, i:i + 1], ident[:, 0:TAB],
                                            start=True, stop=True)
                last.then_inc(cols_turned, 1)

            def experts(l):
                pe.wait_ge(tab_ready, l + 1)
                last = last_tile(pe)

                def turn_x(s):
                    pe.wait_ge(x_loaded[l], (s + 1) * MOVED)
                    xv = x_rows.rearrange("p (q k) -> p k q", k=C)
                    for k in range(C):
                        last = nc.tensor.transpose(ps[:, B_TURN + k // 4, (k % 4) * P:(k % 4 + 1) * P],
                                                   xv[:, k, :], ident[:])
                        if k == 0 and isinstance(s, int) and s == 0:
                            last.then_inc(y_done[l], 1)
                    last.then_inc(x_turned[l], 1)

                def in_parts(out, x, w, first, last, columns):
                    (x_hi, x_lo), (hi, lo) = x, w
                    for i, (xp, wp) in enumerate(((x_hi, hi), (x_hi, lo), (x_lo, hi))):
                        ins = nc.tensor.matmul(out, xp, columns(wp), start=(first and i == 0), stop=(last and i == 2))
                    return ins

                def gate_up(s, peeled):
                    pe.wait_ge(xT_act[l], s + 1)
                    pe.wait_ge(xT_dve[l], s + 1)
                    if not (peeled and s == 0):
                        pe.wait_ge(hid_done[l], s)
                    for c in range(C // 2):
                        if c in (0, 3):
                            b = c // 3
                            pe.wait_ge(b_lo_ready[l], 2 * s + (b + 1))
                            w, used = (b_hi[:, b], b_lo[:, b]), b_used[l]
                        else:
                            a = c - 1
                            pe.wait_ge(a_lo_ready[l], a + 1 if peeled and s == 0 else 4 * s + (a - 1))
                            w, used = (a_hi[:, a], a_lo[:, a]), a_used[l]
                        for i in range(2):
                            k = 2 * c + i
                            ins = in_parts(ps[:, B_GU, :], (xT_hi[:, k, :], xT_lo[:, k, :]), w, k == 0, k == C - 1,
                                           lambda v: v[:, i * 2 * F:(i + 1) * 2 * F])
                        ins.then_inc(used, 1)

                def down(s, number, first):
                    pe.wait_ge(hidT_ready[l], s + 1)
                    if not first:
                        pe.wait_ge(y_copied[l], s)
                    for k in range(FK):
                        pe.wait_ge(a_lo_ready[l], number + (k + 1))
                        for half in range(2):
                            ins = in_parts(ps[:, B_Y + half, :], (hidT_hi[:, k, :], hidT_lo[:, k, :]),
                                           (a_hi[:, k], a_lo[:, k]), k == 0, k == FK - 1,
                                           lambda v: v[:, half * DH:(half + 1) * DH])
                        ins.then_inc(a_used[l] if k == 0 else y_done[l], 1)

                def turn_hid(s):
                    pe.wait_ge(hid_done[l], s + 1)
                    hv = hid.rearrange("p (q k) -> p k q", k=FK)
                    for k in range(FK):
                        last = nc.tensor.transpose(ps[:, B_HIDT, k * P:(k + 1) * P], hv[:, k, :], ident[:])
                    last.then_inc(hid_turned[l], 1)

                def body(s, peeled):
                    gate_up(s, peeled)
                    turn_x(s + 1)
                    if not (peeled and s == 0):
                        down(s - 1, 4 * s, peeled)
                    turn_hid(s)

                pe.wait_ge(z_done, 2 * NT * (l + 1))
                turn_x(0)
                body(0, True)
                body(1, True)
                with pe.Fori(2, last + 1) as s:
                    body(s, False)
                down(last, 4 * last + 2, False)

            for t in range(NT):
                pe.wait_ge(h_loaded[t], 16 if 0 < t < NT - 1 else 32)
                turn_h(t)
            pe.wait_ge(rows_loaded, 16 * 8)
            nc.tensor.transpose(ps[:, 0, 0:NV], vrows, ident[0:NV, 0:NV])
            for i in range(2):
                nc.tensor.transpose(ps[:, 0, NV + i * KBR:NV + (i + 1) * KBR], cfrows[i], ident[0:KBR, 0:KBR])
            for j in range(C):
                n = NS * HA
                last = nc.tensor.transpose(ps[:, 1, j * n:(j + 1) * n], harows[:, j * P:(j + 1) * P], ident[0:n, 0:n])
            last.then_inc(rows_turned, 1)
            pe.wait_ge(rows_act, 1)
            pe.wait_ge(hT_act, NT)
            pe.wait_ge(hT_dve, NT)
            for p in PRODUCTS[0]:
                j, r = p.index // 3, p.index % 3
                if p.index >= 4:
                    pe.wait_ge((a_mixed, c_copied, cv_done)[r], j - 1 if r == 0 else j)
                product_T(0, p, 2 * (p.index % 4), q_done)
            pe.wait_ge(kept, C)
            for j in range(C):
                last = nc.tensor.transpose(ps[0:SA, 4 + j // 4, (j % 4) * P:(j % 4 + 1) * P], keep[:, j, 0:SA], ident[:])
            last.then_inc(state_turned, 1)
            pe.wait_ge(a_mixed, C)
            mixer_tail(0)
            rank(0)
            experts(0)
            for t in range(NT):
                pe.wait_ge(ln_done, NT + t + 1)
                turn_h(2 * NT + t)
            pe.wait_ge(hT_act, 3 * NT)
            pe.wait_ge(hT_dve, 3 * NT)
            tiles = last_tile(pe) + 1
            pe.wait_ge(y_copied[0], tiles)
            def turn_history(i):
                pe.wait_ge(hist_loaded, 16 * (i + 1))
                if i:
                    pe.wait_ge(hist_read, i)
                for j in range(C):
                    last = nc.tensor.transpose(ps[:, 6 + j // 4, (j % 4) * NHB:(j % 4 + 1) * NHB],
                                               hb_rows[:, j * P:(j + 1) * P], ident[0:NHB, 0:NHB])
                last.then_inc(hist_turned, 1)

            def conv_taps(i, j, k0, k1, used):
                if k0 == 0:
                    pe.wait_ge(glu_done, j + 1)
                    pe.wait_ge(b_step, 2 * j + 2)
                    pe.wait_ge(hist_read, 2)
                    if i:
                        pe.wait_ge(pe_conv_read, i)
                u = glu_of[j]
                for k in range(k0, k1):
                    pe.wait_ge(diag_ready, used + 1)
                    d = diag[:, used % DIAGS, :]
                    ends = dict(start=(k == 0), stop=(k == KB - 1))
                    nc.tensor.matmul(ps[:, 6, 0:HALF], d, u[:, k:k + HALF], **ends)
                    nc.tensor.matmul(ps[:, 7, 0:PH], d, u[:, k + HALF:k + NP], skip_group_check=True, **ends)
                    last = nc.tensor.matmul(seqs(ps[:, 7, PH:HALF], DS), d,
                                            seqs(u[:, WB:LB], HB + DS)[:, :, k:k + DS],
                                            start=False, stop=(k == KB - 1), skip_group_check=True)
                    last.then_inc(diag_used, 1)
                    used += 1
                if k1 == KB:
                    pe.wait_ge(diag_used, used)
                    pe.sem_inc(pe_conv_done, 1)
                return used

            used = convs = 0
            for what in PLAN_B:
                j = what[1]
                if what[0] == "C":
                    used = conv_taps(convs, j, what[2], what[3], used)
                    convs += what[3] == KB
                    continue
                for r in range(2):
                    p = PRODUCTS[1][2 * j + r]
                    if p.index >= 3:
                        pe.wait_ge((glu_done, sig_done)[r], j - 1 if r == 0 else j)
                    product_T(1, p, 2 * (p.index % 3), g_done)
                    if j == 0:
                        turn_history(r)
            pe.wait_ge(pe_conv_read, len(PE_CONVS))
            order = DVE_CONVS[:-2] + list(PE_CONVS) + DVE_CONVS[-2:]
            for j in order:
                if j in DVE_CONVS:
                    pe.wait_ge(conv_done, DVE_CONVS.index(j) + 1)
                for a in range(2):
                    last = nc.tensor.matmul(ps[:, 6 + a, 0:HALF], ones[:], mixT[:, j, a * HALF:(a + 1) * HALF],
                                            start=(j == order[0]), stop=(j == order[-1]))
            last.then_inc(sums_done, 1)
            pe.wait_ge(b_step, 2 * C)
            pe.wait_ge(sig_done, C)
            for j in range(C):
                last = nc.tensor.transpose(ps[0:SB, 4 + j // 4, (j % 4) * P:(j % 4 + 1) * P], keep[:, j, 0:SB], ident[:])
            last.then_inc(state_turned, 1)
            for j in range(C):
                if j == 0:
                    pe.wait_ge(mean_ready, 1)
                pe.wait_ge(squared, j + 1)
                for a in range(2):
                    last = nc.tensor.matmul(ps[:, 6 + a, 0:HALF], ones[:], squares[j % 4][:, a * HALF:(a + 1) * HALF],
                                            start=(j == 0), stop=(j == C - 1))
                last.then_inc(squares_used, 1)
            pe.wait_ge(squares_used, C)
            pe.sem_inc(vars_done, 1)
            pe.wait_ge(b_mixed, C)
            mixer_tail(1)
            rank(1)
            experts(1)

        @block.vector
        def _(dve):
            done = [0]

            def step(ins):
                done[0] += 1
                ins.then_inc(step_s, 1)
                dve.wait_ge(step_s, done[0])

            nc.vector.memset(ones[:], 1.0)
            nc.vector.memset(ones16[:], 1.0)
            nc.vector.memset(eps[:], LN_EPS)
            nc.vector.memset(logit[:], 0.0)
            nc.vector.memset(scan[:], 0.0)
            nc.vector.memset(tab[:], 0)
            nc.vector.memset(stage[:], 0.0).then_inc(zeros_made, 1)

            def copy_hT(m):
                t, n = m % NT, ROWS[m % NT]
                if m // NT % 2:
                    dve.wait_ge(h_turned, m + 1)
                    src = ps[:, B_TURN + 1, :].rearrange("p (k n) -> p k n", n=P)[:, :, 0:n]
                    nc.vector.tensor_copy(xT[:, KC:C, 0:n], src).then_inc(hT_dve, 1)
                    return
                dve.wait_ge(hT_act, m + 1)
                for i in range(2):
                    src = ps[:, B_TURN + i, :].rearrange("p (k n) -> p k n", n=P)[:, :, 0:n]
                    at = (slice(None), slice(i * KC, (i + 1) * KC), slice(t * P, t * P + n))
                    last = nc.vector.tensor_tensor(hT_lo[at], src, hT_hi[at].bitcast(F32), ALU.subtract)
                last.then_inc(hT_dve, 1)

            def ln_stats(m):
                t, n = m % NT, ROWS[m % NT]
                for i in range(2):
                    ins = nc.vector.bn_stats(bn[0:n, t, i, :], h[0:n, t, i * DH:(i + 1) * DH])
                step(ins)
                nc.vector.bn_aggr(mv[0:n, t, :], bn[0:n, t].rearrange("p a b -> p (a b)")).then_inc(var_ready, 1)

            def ln_apply(m):
                t, n = m % NT, ROWS[m % NT]
                x = h[0:n, t, :]
                dve.wait_ge(var_ready, m + 1)
                dve.wait_ge(lnp_loaded, 32 * (m // NT + 1))
                nc.vector.scalar_tensor_tensor(out=x, in0=x, scalar=mv[0:n, t, 0:1], in1=lnp[0:n, 0, :],
                                               op0=ALU.subtract, op1=ALU.mult).then_inc(ln_gained, 1)
                dve.wait_ge(sd_ready, m + 1)
                step(nc.vector.reciprocal(sd[0:n, t, 1:2], sd[0:n, t, 0:1]))
                dve.wait_ge(ln_gained, m + 1)
                nc.vector.scalar_tensor_tensor(out=x, in0=x, scalar=sd[0:n, t, 1:2], in1=lnp[0:n, 1, :],
                                               op0=ALU.mult, op1=ALU.add).then_inc(ln_done, 1)

            def read_logits(layer, t):
                n, w = ROWS[t], G + E
                dve.wait_ge(logits_done, NT * layer + t + 1)
                dve.wait_ge(router_loaded, 16 * 4 * DEPTH)
                nc.vector.tensor_tensor(logit[0:n, t, :], ps[0:n, B_LOGIT, t * w:(t + 1) * w],
                                        rb[0:n, layer, :], ALU.add).then_inc(logits_read, 1)

            def mixer_tail(layer):
                for t in range(NT + 2):
                    m = NT * 2 * layer + t
                    if t < NT:
                        n = ROWS[t]
                        dve.wait_ge(h_scaled, NT * 2 * layer + t + 1)
                        for half in range(2):
                            i = 2 * NT * layer + 2 * t + half
                            dve.wait_ge(proj_done, i + 1)
                            x = h[0:n, t, half * DH:(half + 1) * DH]
                            nc.vector.tensor_tensor(x, ps[0:n, 2 * (t % 2) + half, :], x, ALU.add).then_inc(z_done, 1)
                        dve.wait_ge(z_done, 2 * NT * layer + 2 * t + 2)
                        ln_stats(m)
                        ln_apply(m)
                    if t >= 2:
                        read_logits(layer, t - 2)
                    if 1 <= t <= NT:
                        copy_hT(NT * (2 * layer + 1) + t - 1)

            def over(ap, n):
                return ap.unsqueeze(2).to_broadcast([P, NT, n])

            def route(layer):
                dve.wait_ge(logits_read, NT * (layer + 1))
                dve.wait_ge(iota_made, 3)
                dve.wait_ge(consts_made, 3)
                small = [r_small[:, i, :] for i in range(24)]
                gl = logit[:, :, 0:G]
                gmax, gi, gsum, gp, m1, i1, m2, i2, dm, ex, den, w1 = small[0:12]
                assert small[8] is dm and small[9] is ex
                im_g = iota_m[:, 0:G].unsqueeze(1).to_broadcast([P, NT, G])
                im_e = iota_m[:].unsqueeze(1).to_broadcast([P, NT, EG])
                tt = nc.vector.tensor_tensor
                step(nc.vector.tensor_reduce(gmax, gl, AX, ALU.max))
                tt(r_g[:, 0], gl, over(gmax, G), ALU.subtract).then_inc(exp_in, 1)
                step(tt(r_g[:, 1], gl, over(gmax, G), ALU.is_equal))
                step(tt(r_g[:, 1], r_g[:, 1], im_g, ALU.mult))
                step(nc.vector.tensor_reduce(gi, r_g[:, 1], AX, ALU.min))
                step(tt(r_goh[:], im_g, over(gi, G), ALU.is_equal))
                el = logit[:, :, G:G + E].rearrange("p t (g e) -> p t e g", g=G)
                step(tt(r_pick.rearrange("p t (e g) -> p t e g", g=G), el,
                        r_goh[:].unsqueeze(2).to_broadcast([P, NT, EG, G]), ALU.mult))
                sel, q, oh0, sel2, oh1 = [r_e[:, i] for i in range(5)]
                step(nc.vector.tensor_reduce(sel, r_pick.rearrange("p t (e g) -> p t e g", g=G), AX, ALU.add))
                for src, m, i, oh in ((sel, m1, i1, oh0), (sel2, m2, i2, oh1)):
                    step(nc.vector.tensor_reduce(m, src, AX, ALU.max))
                    step(tt(q, src, over(m, EG), ALU.is_equal))
                    step(tt(q, q, im_e, ALU.mult))
                    step(nc.vector.tensor_reduce(i, q, AX, ALU.min))
                    step(tt(oh, im_e, over(i, EG), ALU.is_equal))
                    if src is sel:
                        step(nc.vector.scalar_tensor_tensor(out=sel2, in0=oh, scalar=-3.0e38, in1=sel,
                                                            op0=ALU.mult, op1=ALU.add))
                tt(dm, m2, m1, ALU.subtract).then_inc(exp_in, 1)
                step(tt(r_goh[:], r_goh[:], over(valid[:], G), ALU.mult))
                for c, oh in ((0, oh0), (1, oh1)):
                    ins = tt(pick[:, c].rearrange("p t (g e) -> p t g e", g=G),
                             r_goh[:].unsqueeze(3).to_broadcast([P, NT, G, EG]),
                             oh.unsqueeze(2).to_broadcast([P, NT, G, EG]), ALU.mult)
                step(ins)
                tt(pick16[:], pick[:, 0], pick[:, 1], ALU.add).then_inc(picks_ready, 1)
                dve.wait_ge(exp_out, 2 * layer + 2)
                step(nc.vector.tensor_reduce(gsum, r_g[:, 2], AX, ALU.add))
                step(nc.vector.reciprocal(gp, gsum))
                step(nc.vector.tensor_scalar(den, ex, 1.0, None, ALU.add))
                step(nc.vector.reciprocal(w1, den))
                step(tt(gates[:, 0, :], gp, w1, ALU.mult))
                step(tt(gates[:, 1, :], gates[:, 0, :], ex, ALU.mult))
                dve.wait_ge(ranked, layer + 1)
                H = E // 2
                step(nc.vector.tensor_copy(cnt[:, 0, :], ps[:, B_RANK, NT * E:(NT + 1) * E]))
                step(nc.vector.tensor_scalar(cnt[:, 1, :], cnt[:, 0, :], 0.0, None, ALU.is_gt))
                for i in range(1, NT):
                    step(nc.vector.scalar_tensor_tensor(out=cnt[:, 1, :], in0=cnt[:, 0, :], scalar=float(i * P),
                                                        in1=cnt[:, 1, :], op0=ALU.is_gt, op1=ALU.add))
                nc.vector.memset(cnt[:, 2, 0:EARLY], 1.0)
                nc.vector.tensor_scalar(cnt[:, 2, EARLY:E], cnt[:, 0, EARLY:E], 0.0, None, ALU.is_gt)
                step(nc.vector.tensor_copy(scan[:, 0, 0:2, H:], cnt[:, 0:2]))
                step(nc.vector.tensor_copy(scan[:, 0, 2, H:], cnt[:, 2]))
                src, by = 0, 1
                while by < E:
                    step(tt(scan[:, 1 - src, :, H:], scan[:, src, :, H:], scan[:, src, :, H - by:H + E - by], ALU.add))
                    src, by = 1 - src, 2 * by
                incl = scan[:, src, :, H:]
                step(tt(excl[:], incl, cnt[:], ALU.subtract))
                rankp = ps[:, B_RANK, 0:NT * E].rearrange("p (t e) -> p t e", e=E)
                step(tt(r_pos[:, 0], rankp, excl[:, 0, :].unsqueeze(1).to_broadcast([P, NT, E]), ALU.add))
                for c in range(2):
                    step(tt(r_pos[:, 1], r_pos[:, 0], pick[:, c], ALU.mult))
                    step(nc.vector.tensor_reduce(posf[:, c, :], r_pos[:, 1], AX, ALU.add))
                nc.vector.tensor_copy(posi[:], posf[:].rearrange("p c t -> p (c t)")).then_inc(pos_ready, 1)
                at_p, at_row = iota_p[:, 0:1], iota_p[:, 1:2]
                one = scan[:, 1 - src, 0, H:]
                step(nc.vector.tensor_scalar(one, incl[:, 1, :], at_p, None, ALU.is_le))
                step(nc.vector.scalar_tensor_tensor(out=one, in0=excl[:, 1, :], scalar=at_p, in1=one,
                                                    op0=ALU.is_le, op1=ALU.subtract))
                nc.vector.tensor_copy(tsum[:, 0, :], excl[:, 2, :])
                nc.vector.scalar_tensor_tensor(out=tsum[:, 1, :], in0=excl[:, 1, :], scalar=-float(P),
                                               in1=excl[:, 0, :], op0=ALU.mult, op1=ALU.add)
                nc.vector.scalar_tensor_tensor(out=tsum[:, COLS, :], in0=excl[:, 1, :], scalar=float(P),
                                               in1=cnt[:, 0, :], op0=ALU.mult, op1=ALU.add)
                nc.vector.tensor_scalar(tsum[:, 2, :], incl[:, 2, :], at_p, None, ALU.is_le)
                nc.vector.tensor_scalar(tsum[:, 3, :], incl[:, 2, :], at_p, None, ALU.is_le)
                step(nc.vector.scalar_tensor_tensor(out=tsum[:, 4, :], in0=excl[:, 2, :], scalar=at_p,
                                                    in1=cnt[:, 1, :], op0=ALU.is_le, op1=ALU.mult))
                tt(tsum[:, 0:2, :], tsum[:, 0:2, :], one.unsqueeze(1).to_broadcast([P, 2, E]), ALU.mult)
                step(tt(tsum[:, COLS, :], tsum[:, COLS, :], one, ALU.mult))
                step(nc.vector.tensor_reduce(tcol[:, 0:COLS + 1], tsum[:], AX, ALU.add))
                nc.vector.tensor_scalar(tcol[:, 2:3], tcol[:, 2:3], float(E - 1), None, ALU.min)
                nc.vector.tensor_scalar(tcol[:, 1:2], tcol[:, 1:2], at_row, float(PAIRS), ALU.add, ALU.min)
                rows, some, most = tcol[:, COLS:COLS + 1], tcol[:, COLS + 1:COLS + 2], tcol[:, COLS:COLS + 1]
                nc.vector.tensor_scalar(some, rows, at_row, float(PIECES[1][0]), ALU.subtract, ALU.is_gt)
                step(nc.vector.tensor_scalar(most, rows, at_row, float(PIECES[-1][0]), ALU.subtract, ALU.is_gt))
                step(tt(some, some, most, ALU.add))
                nc.vector.scalar_tensor_tensor(out=tcol[:, 1:2], in0=tcol[:, 1:2], scalar=4.0, in1=some, op0=ALU.mult,
                                               op1=ALU.add).then_inc(cols_ready, 1)
                nc.vector.memset(x_rows, 0.0)
                if layer > 0:
                    dve.wait_ge(weights_ready, SEQ_MIX[layer] + 2)
                for i in range(2):
                    nc.vector.tensor_scalar(tab[:, T_LAST + i:T_LAST + i + 1], incl[0:1, 1, E - 1:E], float(i + 1), None,
                                            ALU.subtract)
                dve.wait_ge(cols_turned, layer + 1)
                records = tab[:, 0:4 * TAB].rearrange("p (i j) -> p j i", j=4)
                turned = ps[0:1, B_LOGIT, 0:COLS * TAB].rearrange("p (i n) -> p i n", i=COLS)
                nc.vector.tensor_copy(records[:, 0, 1:TAB], turned[:, 0, 0:TAB - 1])
                nc.vector.tensor_copy(records[:, 1, 3:TAB], turned[:, 0, 0:TAB - 3])
                nc.vector.tensor_copy(records[:, 2, 4:TAB], turned[:, 1, 0:TAB - 4])
                nc.vector.tensor_copy(records[:, 3, :], turned[:, 1, :])
                nc.vector.tensor_copy(tab[:, T_EXPERT:T_LAST], ps[0:1, B_LOGIT, 2 * TAB:COLS * TAB]).then_inc(tab_ready, 1)

            def experts(l):
                dve.wait_ge(tab_ready, l + 1)
                last, before_last = last_tile(dve), tile_before_last(dve)

                def copy_xT(s):
                    dve.wait_ge(xT_act[l], s + 1)
                    nc.vector.tensor_tensor(xT_lo.rearrange("p (b k) n -> p b (k n)", b=2), ps[:, B_TURN:B_TURN + 2, :],
                                            xT_hi.rearrange("p (b k) n -> p b (k n)", b=2).bitcast(F32),
                                            ALU.subtract).then_inc(xT_dve[l], 1)

                def lo(i, number, chunk):
                    dve.wait_ge(a_hi_ready[l], number + 1)
                    view = as_gu if len(chunk.shape) == 5 else as_down
                    nc.vector.tensor_tensor(view(a_lo[:, i]), chunk, view(a_hi[:, i]).bitcast(F32),
                                            ALU.subtract).then_inc(a_lo_ready[l], 1)

                def copy_y(s, first):
                    dve.wait_ge(y_done[l], s + 2)
                    if not first:
                        dve.wait_ge(y_stored[l], MOVED * s)
                    nc.vector.tensor_copy(y_rows.rearrange("p (i n) -> p i n", i=2), ps[:, B_Y:B_Y + 2, :]).then_inc(y_copied[l], 1)

                def body(s, before, first=False, ends=False):
                    rank, rank_before = record(mybir.EngineType.DVE, s, 2)
                    if before is not None:
                        for k in range(FK):
                            lo(k, 4 * s + k, down_chunk(rank_before, k))
                    dve.wait_ge(silu_done[l], s + 1)
                    if before is not None:
                        dve.wait_ge(hid_turned[l], s)
                    nc.vector.tensor_tensor(hid, silu_sb, ps[:, B_GU, F:2 * F], ALU.mult).then_inc(hid_done[l], 1)
                    copy_xT(s + 1)
                    if not ends:
                        for c in range(2):
                            lo(c, 4 * s + (2 + c), gu_chunk(rank, 1 + c))
                    if before is not None:
                        copy_y(before, first)
                    dve.wait_ge(hidT_act[l], s + 1)
                    nc.vector.tensor_tensor(hidT_lo, ps[:, B_HIDT, 0:F].rearrange("p (k n) -> p k n", k=FK),
                                            hidT_hi.bitcast(F32), ALU.subtract).then_inc(hidT_ready[l], 1)

                rank = rank_of(dve, 0)
                for c in range(2):
                    lo(c, c, gu_chunk(rank, 1 + c))
                copy_xT(0)
                body(0, None)
                body(1, 0, first=True)
                with dve.Fori(2, last) as s:
                    body(s, s - 1)
                body(last, before_last, ends=True)
                rank = rank_of(dve, last)
                for k in range(FK):
                    lo(k, 4 * last + (2 + k), down_chunk(rank, k))
                copy_y(last, False)

            def combine(layer):
                for t in range(NT):
                    n, b = ROWS[t], t % NB
                    uses = sum(1 for u in range(NT) if u % NB == b) * layer + t // NB + 1
                    dve.wait_ge(gathered[b], 32 * uses)
                    dve.wait_ge(h_scaled, NT * (2 * layer + 1) + t + 1)
                    x = h[0:n, t, :]
                    step(nc.vector.scalar_tensor_tensor(out=x, in0=picked[b][0:n, 0, :], scalar=gates[0:n, 0, t:t + 1],
                                                        in1=x, op0=ALU.mult, op1=ALU.add))
                    nc.vector.scalar_tensor_tensor(out=x, in0=picked[b][0:n, 1, :], scalar=gates[0:n, 1, t:t + 1],
                                                   in1=x, op0=ALU.mult, op1=ALU.add).then_inc(combined, 1)
                    dve.wait_ge(combined, NT * layer + t + 1)
                    m = NT * (2 * layer + 1) + t
                    ln_stats(m)
                    ln_apply(m)
                    if layer == 0 and t >= 1:
                        copy_hT(2 * NT + t - 1)
                if layer == 0:
                    copy_hT(3 * NT - 1)

            for t in range(NT):
                copy_hT(t)
            dve.wait_ge(rows_act, 1)
            for i in range(2):
                step(nc.vector.memset(u_in[i][:, 0:HA], 0.0))
            for j in range(C):
                u, c, pair = u_in[j % 2], c_sb[j % 2], 2 * ((3 * j + 1) % 4)
                nc.vector.tensor_copy(seqs(u[:, WA:LA], HA + DS)[:, :, 0:HA],
                                      hist_a[:, j, :].rearrange("p (s r) -> p s r", r=HA))
                dve.wait_ge(c_copied, j + 1)
                dve.wait_ge(q_done, 3 * j + 2)
                nc.vector.tensor_tensor(u[:, HA:HA + HALF], ps[:, pair, 0:HALF], c[:, 0:HALF], ALU.mult)
                nc.vector.tensor_tensor(u[:, HA + HALF:WA], ps[:, pair + 1, 0:PH], c[:, HALF:NP], ALU.mult)
                ins = nc.vector.tensor_tensor(seqs(u[:, WA:LA], HA + DS)[:, :, HA:HA + DS],
                                              seqs(ps[:, pair + 1, PH:HALF], DS), seqs(c[:, NP:T], DS), ALU.mult)
                ins.then_inc(cv_done, 1)
                dve.wait_ge(cv_done, j + 1)
                nc.vector.tensor_copy(keep[:, j, 0:HA], u[:, NP:WA])
                nc.vector.tensor_copy(keep[:, j, HA:SA].rearrange("p (s r) -> p s r", r=HA),
                                      seqs(u[:, WA:LA], HA + DS)[:, :, DS:DS + HA]).then_inc(kept, 1)
                w = LA - HA
                step(nc.vector.tensor_scalar(acc_a, u[:, 0:w], sc_tap(0, j), None, ALU.mult))
                for k in range(1, KA):
                    step(nc.vector.scalar_tensor_tensor(out=acc_a, in0=u[:, k:k + w], scalar=sc_tap(k, j), in1=acc_a,
                                                        op0=ALU.mult, op1=ALU.add))
                dve.wait_ge(q_done, 3 * j + 3)
                pair = 2 * ((3 * j + 2) % 4)
                m = mixT[:, j, :]
                nc.vector.tensor_tensor(m[:, 0:HALF], ps[:, pair, 0:HALF], acc_a[:, 0:HALF], ALU.mult)
                nc.vector.tensor_tensor(m[:, HALF:NP], ps[:, pair + 1, 0:PH], acc_a[:, HALF:NP], ALU.mult)
                sampled = work[:, 2 * LA + 2 * T + WA:2 * LA + 2 * T + LA]
                ins = nc.vector.tensor_tensor(seqs(m[:, NP:T], DS), seqs(ps[:, pair + 1, PH:HALF], DS),
                                              seqs(sampled, HA + DS)[:, :, 0:DS], ALU.mult)
                ins.then_inc(a_mixed, 1)
            mixer_tail(0)
            route(0)
            experts(0)
            combine(0)
            dve.wait_ge(y_stored[0], (last_tile(dve) + 1) * MOVED)
            for i in range(4):
                ins = nc.vector.memset(glu[i][:, 0:HB], 0.0)
            ins.then_inc(zeros_made, 1)
            taken = 0

            def gate(j):
                u, sg, pair = glu_of[j], sig[j % 2], 2 * ((2 * j + 1) % 3)
                dve.wait_ge(sig_done, j + 1)
                dve.wait_ge(g_done, 2 * j + 2)
                for out, in0, in1 in (
                        (u[:, HB:HB + HALF], ps[:, pair, 0:HALF], sg[:, 0:HALF]),
                        (u[:, HB + HALF:WB], ps[:, pair + 1, 0:PH], sg[:, HALF:NP]),
                        (seqs(u[:, WB:LB], HB + DS)[:, :, HB:HB + DS], seqs(ps[:, pair + 1, PH:HALF], DS),
                         seqs(sg[:, NP:T], DS))):
                    ins = nc.vector.scalar_tensor_tensor(out=out, in0=in0, scalar=bias_a(j), in1=in1,
                                                         op0=ALU.add, op1=ALU.mult)
                ins.then_inc(glu_done, 1)
                dve.wait_ge(glu_done, j + 1)
                dve.wait_ge(hist_read, 2)
                nc.vector.tensor_copy(seqs(u[:, WB:LB], HB + DS)[:, :, 0:HB],
                                      seqs(mixT[:, j, 0:NS * HB], HB)).then_inc(b_step, 1)
                nc.vector.tensor_copy(keep[:, j, 0:HB], u[:, NP:WB])
                nc.vector.tensor_copy(keep[:, j, HB:SB].rearrange("p (s r) -> p s r", r=DS),
                                      seqs(u[:, WB:LB], HB + DS)[:, :, HB:HB + DS]).then_inc(b_step, 1)
                dve.wait_ge(b_step, 2 * j + 2)

            for j in range(C):
                gate(j)
                if j in PE_CONVS:
                    continue
                u, m = glu_of[j], mixT[:, j, :]
                for k in range(KB):
                    for out, src in ((m[:, 0:NP], u[:, k:k + NP]),
                                     (seqs(m[:, NP:T], DS), seqs(u[:, WB:LB], HB + DS)[:, :, k:k + DS])):
                        if k == 0:
                            ins = nc.vector.tensor_scalar(out, src, cf_tap(k, j), conv_b(j), ALU.mult, ALU.add)
                        else:
                            dve.wait_ge(conv_step, taken - 1)
                            ins = nc.vector.scalar_tensor_tensor(out=out, in0=src, scalar=cf_tap(k, j), in1=out,
                                                                 op0=ALU.mult, op1=ALU.add)
                        ins.then_inc(conv_step, 1)
                        taken += 1
                dve.wait_ge(conv_step, taken)
                dve.sem_inc(conv_done, 1)
            dve.wait_ge(pe_conv_read, len(PE_CONVS))
            dve.wait_ge(sums_done, 1)
            ins = nc.vector.tensor_scalar(mean_sb.rearrange("p (a n) -> p a n", a=2), ps[:, 6:8, 0:HALF], 1.0 / D, None,
                                          ALU.mult)
            ins.then_inc(mean_ready, 1)
            dve.wait_ge(mean_ready, 1)
            for j in range(C):
                nc.vector.tensor_tensor(mixT[:, j, :], mixT[:, j, :], mean_sb, ALU.subtract).then_inc(centred, 1)
            dve.wait_ge(csd_ready, 1)
            step(nc.vector.reciprocal(mean_sb, rstd_sb))
            dve.wait_ge(squared, C)
            for j in range(C):
                nc.vector.tensor_tensor(mixT[:, j, :], mixT[:, j, :], mean_sb, ALU.mult).then_inc(normed, 1)
            mixer_tail(1)
            route(1)
            experts(1)
            combine(1)


_INS = ['x_prompt', 'x_sample', 'state_conv_a', 'state_conv_b', 'meta_tokens', 'sc_w_in', 'sc_conv_w', 'sc_w_out',
        'cf_w_pw1', 'cf_b_pw1', 'cf_conv_w', 'cf_conv_b', 'cf_ln_g', 'cf_ln_b', 'cf_w_pw2', 'cf_b_pw2',
        'ln1_g', 'ln1_b', 'ln2_g', 'ln2_b', 'rt_group_w', 'rt_group_b', 'rt_expert_w', 'rt_expert_b',
        'moe_w_gate', 'moe_w_up', 'moe_w_down']


def kernel(**inputs):
    import numpy as _np
    import concourse.bacc as _bacc
    from concourse import mybir as _mybir
    from concourse.bass_utils import run_bass_kernel_spmd as _run

    nc = _bacc.Bacc("TRN2", target_bir_lowering=False, num_devices=1)
    arrays, args = {}, []
    for name in _INS:
        a = _np.ascontiguousarray(inputs[name])
        arrays[f"in_{name}_dram"] = a
        args.append(nc.dram_tensor(f"in_{name}_dram", a.shape, _mybir.dt.from_np(a.dtype), kind="ExternalInput").ap())
    xp, xsmp = arrays["in_x_prompt_dram"].shape, arrays["in_x_sample_dram"].shape
    sa, sbs = arrays["in_state_conv_a_dram"].shape, arrays["in_state_conv_b_dram"].shape
    outs = [xp, xsmp, (sa[0], xp[0]) + sa[2:], (sbs[0], xp[0]) + sbs[2:], sa, sbs]
    for i, shape in enumerate(outs):
        args.append(nc.dram_tensor(f"out_{i}_dram", shape, _mybir.dt.float32, kind="ExternalOutput").ap())
    build_decoder_step(nc, *args)
    r = _run(nc, [arrays], core_ids=[0])
    return tuple(r.results[0][f"out_{i}_dram"] for i in range(len(outs)))
```
